# Optimizing a Trainium2 kernel written in Bass

```python
import jax, jax.numpy as jnp
from jax import lax
import numpy as np

D_MODEL = 1024
BATCH = 1
SEQ = 512
DEPTH = 1

CHUNK = 64
HEAD_DIM = 64
N_Q_HEADS = 16
N_KV_HEADS = 2
Q_GROUP = N_Q_HEADS // N_KV_HEADS
WINDOW = 128
N_PREV_CHUNKS = WINDOW // CHUNK - 1
ROPE_THETA = 10000.0
D_ATTN_Q = N_Q_HEADS * HEAD_DIM
D_ATTN_KV = N_KV_HEADS * HEAD_DIM
D_RNN = 1280
N_RNN_BLOCKS = 16
RNN_BLOCK = D_RNN // N_RNN_BLOCKS
CONV_WIDTH = 4
RG_C = 8.0
D_IN = D_ATTN_Q + 2 * D_ATTN_KV + 2 * D_RNN
N_EXPERTS = 32
TOP_K = 4
D_EXPERT = 1024
SWIGLU_LIMIT = 7.0
SWIGLU_ALPHA = 1.702
MOE_BLOCK = 128
NORM_EPS = 1e-6
N_MOD = 6

kernel_name = "hybrid_swa_rglru_moe_block"

def _rmsnorm(x, g):
    xf = x.astype(jnp.float32)
    y = xf * lax.rsqrt(jnp.mean(xf * xf, axis=-1, keepdims=True) + NORM_EPS)
    return (y * g.astype(jnp.float32)).astype(x.dtype)

def _rope(x, positions):
    half = HEAD_DIM // 2
    inv_freq = ROPE_THETA ** (-jnp.arange(half, dtype=jnp.float32) / half)
    ang = positions.astype(jnp.float32)[..., None] * inv_freq
    cos = jnp.cos(ang)[:, :, None, :]
    sin = jnp.sin(ang)[:, :, None, :]
    xf = x.astype(jnp.float32)
    x1, x2 = xf[..., :half], xf[..., half:]
    return jnp.concatenate([x1 * cos - x2 * sin, x2 * cos + x1 * sin], axis=-1).astype(x.dtype)

def _band(t):
    parts = []
    for j in range(N_PREV_CHUNKS, 0, -1):
        parts.append(jnp.pad(t, ((0, 0), (j, 0), (0, 0), (0, 0), (0, 0)))[:, :-j])
    parts.append(t)
    return jnp.concatenate(parts, axis=2)

def _window_attention(q, k, v, sinks):
    B, S = q.shape[:2]
    NC = S // CHUNK
    qc = q.reshape(B, NC, CHUNK, N_KV_HEADS, Q_GROUP, HEAD_DIM)
    kb = _band(k.reshape(B, NC, CHUNK, N_KV_HEADS, HEAD_DIM))
    vb = _band(v.reshape(B, NC, CHUNK, N_KV_HEADS, HEAD_DIM))
    s = jnp.einsum('bnqhgd,bnkhd->bnhgqk', qc, kb,
                   preferred_element_type=jnp.float32) * (HEAD_DIM ** -0.5)
    back = N_PREV_CHUNKS - jnp.arange(kb.shape[2]) // CHUNK
    valid = jnp.arange(NC)[:, None] >= back[None, :]
    s = jnp.where(valid[None, :, None, None, None, :], s, -1e30)
    sink = sinks.astype(jnp.float32).reshape(N_KV_HEADS, Q_GROUP)[None, None, :, :, None, None]
    m = jnp.maximum(s.max(axis=-1, keepdims=True), sink)
    p = jnp.exp(s - m)
    p = p / (p.sum(axis=-1, keepdims=True) + jnp.exp(sink - m))
    o = jnp.einsum('bnhgqk,bnkhd->bnqhgd', p.astype(vb.dtype), vb)
    return o.reshape(B, S, D_ATTN_Q)

def _causal_conv(x, w, b):
    S = x.shape[1]
    xp = jnp.pad(x, ((0, 0), (CONV_WIDTH - 1, 0), (0, 0)))
    return sum(xp[:, j:j + S] * w[j] for j in range(CONV_WIDTH)) + b

def _rg_lru(x, w_a, b_a, w_x, b_x, lam):
    B, S, _ = x.shape
    xb = x.reshape(B, S, N_RNN_BLOCKS, RNN_BLOCK)
    r = jax.nn.sigmoid((jnp.einsum('bsnk,nkj->bsnj', xb, w_a) + b_a).astype(jnp.float32)).reshape(B, S, D_RNN)
    i = jax.nn.sigmoid((jnp.einsum('bsnk,nkj->bsnj', xb, w_x) + b_x).astype(jnp.float32)).reshape(B, S, D_RNN)
    log_a = -RG_C * r * jax.nn.softplus(-lam.astype(jnp.float32))
    a = jnp.exp(log_a)
    u = jnp.sqrt(-jnp.expm1(2.0 * log_a)) * i * x.astype(jnp.float32)

    def combine(left, right):
        a1, b1 = left
        a2, b2 = right
        return a1 * a2, a2 * b1 + b2

    _, h = lax.associative_scan(combine, (a, u), axis=1)
    return h.astype(x.dtype)

def _moe(h, w_router, b_router, w_e1, b_e1, w_e2, b_e2):
    B, S, D = h.shape
    T = B * S
    TK = T * TOP_K
    xf = h.reshape(T, D)
    logits = (xf @ w_router + b_router).astype(jnp.float32)
    top_val, top_idx = lax.top_k(logits, TOP_K)
    top_w = jax.nn.softmax(top_val, axis=-1)
    flat_e = top_idx.reshape(TK).astype(jnp.int32)
    order = jnp.argsort(flat_e).astype(jnp.int32)
    sorted_e = flat_e[order]
    counts = jnp.zeros((N_EXPERTS,), jnp.int32).at[flat_e].add(1)
    padded = (counts + MOE_BLOCK - 1) // MOE_BLOCK * MOE_BLOCK
    pad_end = jnp.cumsum(padded)
    pad_start = pad_end - padded
    start = jnp.cumsum(counts) - counts
    dest = pad_start[sorted_e] + jnp.arange(TK, dtype=jnp.int32) - start[sorted_e]
    n_blocks = -(-TK // MOE_BLOCK) + N_EXPERTS
    rows = n_blocks * MOE_BLOCK
    row_tok = jnp.full((rows,), T, jnp.int32).at[dest].set(order // TOP_K)
    xpad = jnp.concatenate([xf, jnp.zeros((1, D), xf.dtype)], axis=0)
    xrows = xpad[row_tok].reshape(n_blocks, MOE_BLOCK, D)
    block_e = jnp.minimum(
        jnp.searchsorted(pad_end, jnp.arange(n_blocks, dtype=jnp.int32) * MOE_BLOCK, side='right'),
        N_EXPERTS - 1)

    def expert_block(args):
        xb, e = args
        gu = xb @ w_e1[e] + b_e1[e]
        gate = jnp.minimum(gu[:, :D_EXPERT], SWIGLU_LIMIT)
        up = jnp.clip(gu[:, D_EXPERT:], -SWIGLU_LIMIT, SWIGLU_LIMIT)
        act = (up + 1) * (gate * jax.nn.sigmoid(SWIGLU_ALPHA * gate))
        return act @ w_e2[e] + b_e2[e]

    yrows = lax.map(expert_block, (xrows, block_e)).reshape(rows, D)
    dest_by_assign = jnp.zeros((TK,), jnp.int32).at[order].set(dest).reshape(T, TOP_K)
    y = jnp.einsum('tkd,tk->td', yrows[dest_by_assign], top_w.astype(yrows.dtype))
    return y.reshape(B, S, D)

def setup_inputs(seed: int = 0) -> dict:
    key = jax.random.key(seed)
    ks = jax.random.split(key, 32)
    f32 = jnp.float32

    def nrm(k, shape, scale):
        return jax.random.normal(k, shape, f32) * scale

    x = jax.random.normal(ks[0], (BATCH, SEQ, D_MODEL), f32)
    c = jax.random.normal(ks[1], (BATCH, D_MODEL), f32)
    offset = jax.random.randint(ks[2], (BATCH, 1), 0, 4096, jnp.int32)
    positions = offset + jnp.arange(SEQ, dtype=jnp.int32)[None, :]
    u = jax.random.uniform(ks[3], (DEPTH, D_RNN), f32, 0.9, 0.999)
    p = u ** (1.0 / RG_C)
    rg_lambda = jnp.log(p) - jnp.log1p(-p)
    return {
        "x": x,
        "c": c,
        "positions": positions,
        "w_ada": nrm(ks[4], (DEPTH, D_MODEL, N_MOD * D_MODEL), 0.5 * D_MODEL ** -0.5),
        "b_ada": nrm(ks[5], (DEPTH, N_MOD * D_MODEL), 0.02),
        "g_pre_mix": 1.0 + nrm(ks[6], (DEPTH, D_MODEL), 0.1),
        "g_post_mix": 1.0 + nrm(ks[7], (DEPTH, D_MODEL), 0.1),
        "g_pre_ffn": 1.0 + nrm(ks[8], (DEPTH, D_MODEL), 0.1),
        "g_post_ffn": 1.0 + nrm(ks[9], (DEPTH, D_MODEL), 0.1),
        "w_in": nrm(ks[10], (DEPTH, D_MODEL, D_IN), D_MODEL ** -0.5),
        "sinks": nrm(ks[11], (DEPTH, N_Q_HEADS), 1.0),
        "conv_w": nrm(ks[12], (DEPTH, CONV_WIDTH, D_RNN), CONV_WIDTH ** -0.5),
        "conv_b": nrm(ks[13], (DEPTH, D_RNN), 0.02),
        "w_rg_a": nrm(ks[14], (DEPTH, N_RNN_BLOCKS, RNN_BLOCK, RNN_BLOCK), RNN_BLOCK ** -0.5),
        "b_rg_a": nrm(ks[15], (DEPTH, N_RNN_BLOCKS, RNN_BLOCK), 0.02),
        "w_rg_x": nrm(ks[16], (DEPTH, N_RNN_BLOCKS, RNN_BLOCK, RNN_BLOCK), RNN_BLOCK ** -0.5),
        "b_rg_x": nrm(ks[17], (DEPTH, N_RNN_BLOCKS, RNN_BLOCK), 0.02),
        "rg_lambda": rg_lambda,
        "w_branch_attn": nrm(ks[18], (DEPTH, D_ATTN_Q, D_MODEL), D_ATTN_Q ** -0.5),
        "w_branch_rnn": nrm(ks[19], (DEPTH, D_RNN, D_MODEL), D_RNN ** -0.5),
        "w_merge_gate": nrm(ks[20], (DEPTH, D_MODEL, 2 * D_MODEL), D_MODEL ** -0.5),
        "b_merge_gate": nrm(ks[21], (DEPTH, 2 * D_MODEL), 0.02),
        "w_out": nrm(ks[22], (DEPTH, D_MODEL, D_MODEL), D_MODEL ** -0.5),
        "w_router": nrm(ks[23], (DEPTH, D_MODEL, N_EXPERTS), D_MODEL ** -0.5),
        "b_router": nrm(ks[24], (DEPTH, N_EXPERTS), 0.01),
        "w_e1": nrm(ks[25], (DEPTH, N_EXPERTS, D_MODEL, 2 * D_EXPERT), D_MODEL ** -0.5),
        "b_e1": nrm(ks[26], (DEPTH, N_EXPERTS, 2 * D_EXPERT), 0.02),
        "w_e2": nrm(ks[27], (DEPTH, N_EXPERTS, D_EXPERT, D_MODEL), D_EXPERT ** -0.5),
        "b_e2": nrm(ks[28], (DEPTH, N_EXPERTS, D_MODEL), 0.02),
    }

def reference(x, c, positions, w_ada, b_ada, g_pre_mix, g_post_mix, g_pre_ffn, g_post_ffn,
              w_in, sinks, conv_w, conv_b, w_rg_a, b_rg_a, w_rg_x, b_rg_x, rg_lambda,
              w_branch_attn, w_branch_rnn, w_merge_gate, b_merge_gate, w_out,
              w_router, b_router, w_e1, b_e1, w_e2, b_e2):
    B, S, _ = x.shape
    splits = [D_ATTN_Q, D_ATTN_Q + D_ATTN_KV, D_ATTN_Q + 2 * D_ATTN_KV, D_ATTN_Q + 2 * D_ATTN_KV + D_RNN]
    for l in range(DEPTH):
        mod = jax.nn.silu(c) @ w_ada[l] + b_ada[l]
        shift_m, scale_m, gate_m, shift_f, scale_f, gate_f = [t[:, None, :] for t in jnp.split(mod, N_MOD, axis=-1)]

        h = _rmsnorm(x, g_pre_mix[l]) * (1 + scale_m) + shift_m
        q, k, v, xr, gr = jnp.split(h @ w_in[l], splits, axis=-1)
        q = _rope(q.reshape(B, S, N_Q_HEADS, HEAD_DIM), positions)
        k = _rope(k.reshape(B, S, N_KV_HEADS, HEAD_DIM), positions)
        v = v.reshape(B, S, N_KV_HEADS, HEAD_DIM)
        attn = _window_attention(q, k, v, sinks[l])
        xc = _causal_conv(xr, conv_w[l], conv_b[l])
        rnn = _rg_lru(xc, w_rg_a[l], b_rg_a[l], w_rg_x[l], b_rg_x[l], rg_lambda[l]) * jax.nn.gelu(gr)
        g_attn, g_rnn = jnp.split(jax.nn.sigmoid(h @ w_merge_gate[l] + b_merge_gate[l]), 2, axis=-1)
        mixed = (g_attn * (attn @ w_branch_attn[l]) + g_rnn * (rnn @ w_branch_rnn[l])) @ w_out[l]
        x = x + gate_m * _rmsnorm(mixed, g_post_mix[l])

        h = _rmsnorm(x, g_pre_ffn[l]) * (1 + scale_f) + shift_f
        y = _moe(h, w_router[l], b_router[l], w_e1[l], b_e1[l], w_e2[l], b_e2[l])
        x = x + gate_f * _rmsnorm(y, g_post_ffn[l])
    return x


_drawn_inputs = setup_inputs


def setup_inputs(seed=0):
    import zlib

    import numpy as np

    out = dict(_drawn_inputs(seed))
    spreads = {}
    factors = {'sinks': 6.226,
     'b_rg_a': 28.17,
     'b_rg_x': 7.419,
     'b_merge_gate': 6.745,
     'b_e1': 8.0,
     'b_e2': 8.0,
     'b_router': 2.797}
    for name, (base, spread) in spreads.items():
        noise = np.random.default_rng([zlib.crc32(name.encode()), seed]).standard_normal(out[name].shape)
        drawn = base * np.exp(spread * noise) if base else spread * noise
        out[name] = __import__('jax').numpy.asarray(drawn.astype(out[name].dtype))
    for name, factor in factors.items():
        out[name] = (out[name] * factor).astype(out[name].dtype)
    return out
```

```python
from contextlib import ExitStack

import concourse.bass as bass
from concourse import mybir

ALU = mybir.AluOpType
ACT = mybir.ActivationFunctionType
F32 = mybir.dt.float32
F32R = mybir.dt.float32r
BF16 = mybir.dt.bfloat16
I32 = mybir.dt.int32
U32 = mybir.dt.uint32
AX_X = mybir.AxisListType.X

P = 128
KB = 1024
SEQ, D = 512, 1024
KT = D // P
TT = SEQ // P
CHUNK, HD, NQ, NKV = 64, 64, 16, 2
NC = SEQ // CHUNK
D_RNN, RB, NRB = 1280, 80, 16
MT = D_RNN // P
CONV = 4
NE, TOPK, DE = 32, 4, 1024
LIMIT, ALPHA = 7.0, 1.702
SIG_LIMIT = 0.9999933068838914
EPS = 1e-6
N_OVER = SEQ * TOPK // P
N_BLOCKS = NE + N_OVER
N_FIRST = NE - 1
N_LAST = N_BLOCKS - N_FIRST
NOWHERE = 1 << 20
QCOL, KCOL, VCOL, XCOL = 0, 1024, 1152, 1280
GCOL = XCOL + D_RNN
W = 256
CH = 2048
RS = 4
MS = 12
HS = 4

R_CONVW, R_BMG, R_GPM, R_C, R_CONVB, R_BA, R_BX, R_LAM, R_END = 0, 40, 56, 64, 72, 82, 92, 102, 112


def gate_pairs(m):
    lo, hi = (m * P // RB) * RB, -(-((m + 1) * P) // RB) * RB
    return list(range(lo // P, (hi - 1) // P + 1))


PAIRS = [(k, m) for m in range(MT) for k in gate_pairs(m)]
READY = [[m for m in range(MT) if max(gate_pairs(m)) // 2 == j] for j in range(MT // 2)]


def gate_pieces():
    out = []
    for q, (k, m) in enumerate(PAIRS):
        for b in range(NRB):
            r0, r1 = max(b * RB, k * P), min((b + 1) * RB, (k + 1) * P)
            c0, c1 = max(b * RB, m * P), min((b + 1) * RB, (m + 1) * P)
            if r0 < r1 and c0 < c1:
                out.append((q, b, r0, r1, c0, c1))
    return out


GATE_PIECES = gate_pieces()


def stream_items():
    ada = [[("ada", part, k) for k in range(KT)] for part in range(3)]
    items = list(ada[0])
    for j in range(MT // 2):
        items.append(("in", XCOL + W * j))
        if ada[1]:
            items.append(ada[1].pop(0))
        items.append(("in", GCOL + W * j))
        if ada[1]:
            items.append(ada[1].pop(0))
    for p in range(4):
        items.append(("mg", D + W * p))
        items.append(("br", p, 0))
        items.append(ada[2].pop(0))
        items.append(("br", p, 1))
        items.append(ada[2].pop(0))
    items.append(("in", KCOL))
    items += [("in", QCOL + W * p) for p in range(4)]
    for p in range(4):
        items += [("mg", W * p), ("ba", p)]
    items += [("out", p) for p in range(4)]
    return items


STREAM = stream_items()
WEIGHTS = [n for n, it in enumerate(STREAM) if it[0] != "ada"]
ADAS = [n for n, it in enumerate(STREAM) if it[0] == "ada"]
W_MIX = len(WEIGHTS)
W_RNN, W_BR, W_KV, W_Q, W_BA, W_OUT = 0, 10, 22, 23, 27, 35
assert W_OUT + 4 == W_MIX and (W_MIX + 1) % HS == 0


def hi_slot(w):
    return (w + 1) % HS


class Steps:

    def __init__(self, eng, sem):
        self.eng, self.sem, self.n, self.at = eng, sem, 0, None

    def __call__(self, ins):
        ins.then_inc(self.sem, 1)
        self.n += 1
        return ins

    def wait(self, back=0):
        n = self.n - back
        self.eng.wait_ge(self.sem, n if self.at is None else self.at + n)

    def link(self, ins):
        self(ins)
        self.wait()


def hybrid_block(nc, a, out):
    with ExitStack() as ctx:
        def sem(name):
            return ctx.enter_context(nc.semaphore(name))

        base = -(-nc.sbuf_base // 64) * 64
        end = nc.sbuf_usable_end
        top = [base]

        def put(name, shape, dt, off):
            return nc.alloc_sbuf_tensor_at(name, shape, dt, offset=off)

        def keep(name, shape, dt=F32):
            size = 2 if dt == BF16 else 4
            for s in shape[1:]:
                size *= s
            t = put(name, shape, dt, top[0])
            top[0] += -(-size // 32) * 32
            return t

        ident = keep("ident", [P, P])
        ones = keep("ones", [P, P])
        iota_f = keep("iota_f", [P, P])
        before = keep("before", [P, P])
        cols = keep("cols", [P, R_END])
        bcol = keep("bcol", [P, 36])
        scol = keep("scol", [P, KT])
        sp4 = keep("sp4", [P, 2, MT])
        modc = keep("modc", [P, 2, KT])
        small = keep("small", [P, 64])
        sink = keep("sink", [P, 8])
        eps = keep("eps", [P, 1])
        ticks = keep("ticks", [P, 4])
        freq = keep("freq", [P, 1])
        topw = keep("topw", [P, TT, TOPK])
        ssq = keep("ssq", [P, 4, TT])
        tok_i = keep("tok_i", [P, N_BLOCKS + 1], I32)
        asg_i = keep("asg_i", [P, N_BLOCKS + 1], I32)
        over_i = keep("over_i", [P, N_LAST + 2], I32)
        asgv = keep("asgv", [P, TOPK, TT])
        idx_now = keep("idx_now", [P, 2], I32)
        gate_m = keep("gate_m", [P, D])
        gate_f = keep("gate_f", [P, D])
        slots_at = top[0]
        hi_at = slots_at + RS * CH * 4
        zone = hi_at + HS * CH * 4
        assert zone + 131 * KB + 64 <= end

        def z(name, shape, dt, kb):
            return put(name, shape, dt, zone + int(kb * KB))

        slot_off = [slots_at + i * CH * 4 for i in range(RS)] + [zone + i * CH * 4 for i in range(MS - RS)]
        raw = [put(f"raw{i}", [P, CH], F32, slot_off[i]) for i in range(MS)]
        lo = [put(f"lo{i}", [P, CH], F32R, slot_off[i]) for i in range(MS)]
        hi = [put(f"hi{i}", [P, CH], F32R, hi_at + i * CH * 4) for i in range(HS)]

        hT = [z(f"hT{i}", [P, KT, SEQ], F32R, 16 * i) for i in range(2)]
        rnnT = [z(f"rnnT{i}", [P, MT, SEQ], F32R, 32 + 20 * i) for i in range(2)]
        mix = z("mix", [P, KT, SEQ], F32, 72)
        attnT = [z(f"attnT{i}", [P, KT, SEQ], F32R, 88 + 16 * i) for i in range(2)]
        xt = z("xt", [P, TT, D], F32, 88)
        rows = z("rows", [P, P], F32, 104)
        htmp = z("htmp", [P, 2, SEQ], F32, 106)
        xjunk = z("xjunk", [P, D], F32, 110)
        acc = [z("acc0", [P, 2 * D], F32, 114), z("acc1", [P, 2 * D], F32, 114), z("acc2", [P, 2 * D], F32, 92)]
        gw = z("gw", [P, 2, len(PAIRS), P], F32, 88)
        xc = z("xc", [P, 4, SEQ], F32, 72)
        th_a, th_i, dec, t_om = (z(n, [P, SEQ], F32, 80 + 2 * i) for i, n in enumerate(("th_a", "th_i", "dec", "t_om")))
        sq = z("sq", [P, SEQ], F32, 122)
        gr = z("gr", [P, SEQ], F32, 124)
        g2 = z("g2", [P, SEQ], F32, 126)
        xrp = z("xrp", [P, SEQ + 4], F32, 128)
        gate_s = z("gate_s", [P, 2, SEQ], F32, 88)
        shift_f = z("shift_f", [P, D], F32, 123)
        scale_f = z("scale_f", [P, D], F32, 127)
        cos = z("cos", [P, SEQ], F32, 32)
        sin = z("sin", [P, SEQ], F32, 34)
        qbd = z("qbd", [P, 4, NC, 2, CHUNK], F32, 36)
        kT = z("kT", [P, NKV, SEQ], F32, 52)
        vb = z("vb", [P, NC - 1, NKV, 2, HD], F32, 56)
        swp = z("swp", [P, SEQ], F32, 120)
        rot = z("rot", [P, SEQ], F32, 68)
        prob = z("prob", [P, 2, 4, P], F32, 64)
        probT = z("probT", [P, 2, 4, P], F32, 68)
        kpos = z("kpos", [P, SEQ], I32, 70)
        gate_a = z("gate_a", [P, 2, SEQ], F32, 64)
        mtmp = z("mtmp", [P, 2, SEQ], F32, 68)
        mrgT = [z(f"mrgT{i}", [P, KT, SEQ], F32R, 32 + 16 * i) for i in range(2)]
        x2 = z("x2", [P, TT, D], F32, 64)
        h2 = z("h2", [P, 2, D], F32, 80)
        hfT = z("hfT", [P, KT, P], F32, 88)
        junk = z("junk", [P, D], F32, 92)
        btab = z("btab", [NE, 3 * DE], F32, 96)
        bpart = z("bpart", [3 * NE, 3 * DE], BF16, 108)
        wr = z("wr", [P, KT, NE], F32, 114)
        brt = z("brt", [P, NE], F32, 115)
        bt16 = z("bt16", [NE, 3 * DE], BF16, 88)
        top8 = z("top8", [P, TT, 8], F32, 104)
        idx8 = z("idx8", [P, TT, 8], U32, 104.25)
        idxf = z("idxf", [P, TT, 8], F32, 104.5)
        pick = z("pick", [P, 2, TOPK * TT], F32, 104.75)
        over_f = z("over_f", [P, N_LAST + 2], F32, 105)
        ohe = z("ohe", [P, 2, TOPK * TT, NE], F32, 118)
        oh_slot = z("oh_slot", [P, TOPK * TT, P], F32, 64)
        oh_blk = z("oh_blk", [P, TOPK * TT, 64], F32, 72)
        tabf = z("tabf", [P, 2, 64], F32, 76)
        route = z("route", [P, 40, NE], F32, 98)
        xg = z("xg", [P, D], F32, 64)
        xT = [z(f"xT{i}", [P, KT, P], F32R, 68 + 4 * i) for i in range(2)]
        sg, gmin, ucl = (z(n, [P, 512], F32, 76 + 2 * i) for i, n in enumerate(("sg", "gmin", "ucl")))
        act_h = z("act_h", [P, 2, 512], F32, 82)
        aT = [z(f"aT{i}", [P, KT, P], F32R, 86 + 4 * i) for i in range(2)]
        ysb = z("ysb", [P, D], F32, 94)
        sel = z("sel", [3 * NE, P], BF16, 116)
        onehot = z("onehot", [3 * NE, NE], BF16, 117)
        yk = z("yk", [P, 2, TOPK, D], F32, 0)
        x2t = z("x2t", [P, 2, D], F32, 32)
        comb = z("comb", [P, 2, D], F32, 40)
        tjunk = z("tjunk", [P, D], F32, 48)

        ps = ctx.enter_context(nc.psum_tensor("ps", [P, 8, 512], F32))

        h2_d = nc.dram_tensor("h2_d", (SEQ, D), F32).ap()
        x2_d = nc.dram_tensor("x2_d", (SEQ, D), F32).ap()
        yk_d = nc.dram_tensor("yk_d", (SEQ * TOPK, D), F32).ap()

        chunk_in = [sem(f"chunk_in{i}") for i in range(MS)]
        hi_done = sem("hi_done")
        split_done = sem("split_done")
        chunk_used = sem("chunk_used")
        ada_used = sem("ada_used")
        small_in = sem("small_in")
        rows_in = sem("rows_in")
        x_in = sem("x_in")
        acc_in = [sem(f"acc_in{i}") for i in range(3)]
        acc_zero = sem("acc_zero")
        consts = sem("consts")
        gw_zero = sem("gw_zero")
        gw_in = sem("gw_in")
        pool_step = sem("pool_step")
        act_step = sem("act_step")
        dve_step = sem("dve_step")
        cols_ps = sem("cols_ps")
        cols_done = sem("cols_done")
        cexp = sem("cexp")
        scol_done = sem("scol_done")
        ssq_done = sem("ssq_done")
        rms_done = sem("rms_done")
        xn_done = sem("xn_done")
        mod_ps = sem("mod_ps")
        mod_done = sem("mod_done")
        tr_done = sem("tr_done")
        htmp_done = sem("htmp_done")
        hT_hi = sem("hT_hi")
        hT_done = sem("hT_done")
        sp_exp = sem("sp_exp")
        sp_done = sem("sp_done")
        x_ps = sem("x_ps")
        xrp_done = sem("xrp_done")
        conv_done = sem("conv_done")
        g_ps = sem("g_ps")
        gates_ps = sem("gates_ps")
        gates_read = sem("gates_read")
        a_done = sem("a_done")
        om_done = sem("om_done")
        sqrt_done = sem("sqrt_done")
        g2_done = sem("g2_done")
        inner_done = sem("inner_done")
        gelu_th = sem("gelu_th")
        rnn_done = sem("rnn_done")
        rnn_hi = sem("rnn_hi")
        rnn_lo = sem("rnn_lo")
        bg_ps = sem("bg_ps")
        bg_done = sem("bg_done")
        bp_ps = sem("bp_ps")
        ag_ps = sem("ag_ps")
        ap_ps = sem("ap_ps")
        bm_done = sem("bm_done")
        pos_in = sem("pos_in")
        ang_done = sem("ang_done")
        trig_done = sem("trig_done")
        kv_ps = sem("kv_ps")
        q_ps = sem("q_ps")
        swp_done = sem("swp_done")
        rope_done = sem("rope_done")
        kT_done = sem("kT_done")
        v_done = sem("v_done")
        qbd_zero = sem("qbd_zero")
        s_ps = sem("s_ps")
        m_done = sem("m_done")
        e_done = sem("e_done")
        p_done = sem("p_done")
        pT_ps = sem("pT_ps")
        pT_done = sem("pT_done")
        o_ps = sem("o_ps")
        o_hi = sem("o_hi")
        o_done = sem("o_done")
        mrg_sum = sem("mrg_sum")
        mrg_hi = sem("mrg_hi")
        mrg_done = sem("mrg_done")
        e_ssq = sem("e_ssq")
        e_rms = sem("e_rms")
        xe_in = sem("xe_in")
        x2_done = sem("x2_done")
        h2_done = sem("h2_done")
        h2_out = [sem(f"h2_out{i}") for i in range(TT)]
        x2_out = sem("x2_out")
        h2_tr = sem("h2_tr")
        hfT_done = sem("hfT_done")
        lg_ps = sem("lg_ps")
        lg_done = sem("lg_done")
        bt_in = sem("bt_in")
        bpart_done = sem("bpart_done")
        mask_done = sem("mask_done")
        rank_ps = sem("rank_ps")
        wexp = sem("wexp")
        wsub = sem("wsub")
        oh_done = sem("oh_done")
        tab_ps = sem("tab_ps")
        tab_done = sem("tab_done")
        xg_in = sem("xg_in")
        xg_zero = sem("xg_zero")
        xT_ps = sem("xT_ps")
        xT_hi = sem("xT_hi")
        xT_done = sem("xT_done")
        sel_done = sem("sel_done")
        glu_step = sem("glu_step")
        sg_done = sem("sg_done")
        glu_done = sem("glu_done")
        aT_ps = sem("aT_ps")
        aT_hi = sem("aT_hi")
        aT_done = sem("aT_done")
        y_done = sem("y_done")
        y_out = sem("y_out")
        ysb_free = sem("ysb_free")
        gpost_in = sem("gpost_in")
        idx_done = sem("idx_done")
        moe_done = sem("moe_done")
        yk_in = [sem(f"yk_in{i}") for i in range(2)]
        comb_done = sem("comb_done")
        t_ssq = sem("t_ssq")
        t_rms = sem("t_rms")
        fin_done = sem("fin_done")
        out_done = [sem(f"out_done{i}") for i in range(2)]
        tail_step = sem("tail_step")

        w_in, w_mg, w_ba, w_br, w_out = (a[n][0] for n in ("w_in", "w_merge_gate", "w_branch_attn", "w_branch_rnn", "w_out"))
        w_e1, w_e2 = a["w_e1"], a["w_e2"]
        x_tok = a["x"][0].rearrange("(i p) d -> p i d", p=P)

        def chunk_src(it):
            if it[0] == "ada":
                return a["w_ada"][0][it[2] * P:(it[2] + 1) * P, it[1] * CH:(it[1] + 1) * CH], None
            if it[0] == "in":
                return w_in[:, it[1]:it[1] + W].rearrange("(k p) n -> p k n", p=P), KT
            if it[0] == "mg":
                return w_mg[:, it[1]:it[1] + W].rearrange("(k p) n -> p k n", p=P), KT
            if it[0] == "ba":
                return w_ba[:, it[1] * W:(it[1] + 1) * W].rearrange("(k p) n -> p k n", p=P), KT
            if it[0] == "br":
                h = MT // 2
                return w_br[it[2] * h * P:(it[2] + 1) * h * P, it[1] * W:(it[1] + 1) * W].rearrange("(k p) n -> p k n", p=P), h
            return w_out[it[1] * 2 * P:(it[1] + 1) * 2 * P, :].rearrange("(k p) n -> p k n", p=P), 2

        def tile_ready(eng, first, t, w):
            if t % 2 == 0:
                eng.wait_ge(first, t // 2 + 1)
            else:
                eng.wait_ge(chunk_used, w + 1)

        def words(it):
            return (MT // 2) * W if it[0] == "br" else CH

        last_use = {}
        for n in range(len(STREAM)):
            last_use[n % RS] = n
        mix_uses = [len([n for n in range(len(STREAM)) if n % RS == i]) if i < RS else 0 for i in range(MS)]

        def slot_free(eng, n):
            if STREAM[n][0] == "ada":
                eng.wait_ge(ada_used, ADAS.index(n) + 1)
            else:
                eng.wait_ge(chunk_used, WEIGHTS.index(n) + 1)

        def expert_src(e, i):
            if i < 8:
                half, what, kk = i // 4, (i // 2) % 2, i % 2
                c0 = what * DE + half * 512
                return w_e1[0, e, kk * 512:(kk + 1) * 512, c0:c0 + 512].rearrange("o (k p) n -> p (o k) n", p=P)
            r0 = (i - 8) * 256
            return w_e2[0, e, r0:r0 + 256, :].rearrange("o (k p) n -> p (o k) n", p=P)

        def expert_dst(i):
            return raw[i][:, :].rearrange("p (k n) -> p k n", k=4 if i < 8 else 2)

        block = ctx.enter_context(nc.Block())

        @block.sync
        def _(sp):
            for n, it in enumerate(STREAM):
                if n >= RS:
                    slot_free(sp, n - RS)
                src, k = chunk_src(it)
                dst = raw[n % RS][:, 0:words(it)]
                if k is not None:
                    dst = dst.rearrange("p (k n) -> p k n", k=k)
                sp.dma_start(dst, src).then_inc(chunk_in[n % RS], 16)

            for i in range(MS):
                if i < RS:
                    slot_free(sp, last_use[i])
                elif i == RS:
                    sp.wait_ge(chunk_used, W_BA + 7)
                elif i == 8:
                    sp.wait_ge(chunk_used, W_MIX)
                sp.dma_start(expert_dst(i), expert_src(bass.DynSlice(0, 1), i)).then_inc(chunk_in[i], 16)
            def load_expert(e, b):
                for i in range(MS):
                    sp.wait_ge(chunk_used, b * MS + (W_MIX - MS + i + 1))
                    sp.dma_start(expert_dst(i), expert_src(bass.DynSlice(e, 1), i)).then_inc(chunk_in[i], 16)

            with sp.Fori(1, N_FIRST) as b:
                load_expert(b, b)
            sp.wait_ge(tab_done, 1)
            n_last = sp.value_load(over_i[0:1, N_LAST + 1:N_LAST + 2], min_val=1, max_val=N_LAST)
            with sp.Fori(0, N_LAST) as t:
                with sp.If(n_last > t):
                    e = sp.value_load(over_i[0:1, bass.DynSlice(t, 1)], min_val=0, max_val=NE - 1)
                    load_expert(e, t + N_FIRST)
            yk_rows = yk_d.rearrange("(i p k) d -> i p k d", p=P, k=TOPK)
            out_tok = out[0].rearrange("(i p) d -> i p d", p=P)
            x2_tok = x2_d.rearrange("(i p) d -> i p d", p=P)
            sp.wait_ge(moe_done, 1)
            sp.wait_ge(x2_out, 16)
            for i in range(2):
                sp.dma_start(yk[:, i, :, :], yk_rows[i]).then_inc(yk_in[i], 16)
                sp.dma_start(x2t[:, i, :], x2_tok[i]).then_inc(yk_in[i], 16)
            for i in range(TT):
                sp.wait_ge(fin_done, i + 1)
                sp.dma_start(out_tok[i], comb[:, i % 2, :]).then_inc(out_done[i % 2], 16)
                if i + 2 < TT:
                    sp.dma_start(yk[:, i % 2, :, :], yk_rows[i + 2]).then_inc(yk_in[i % 2], 16)
                    sp.dma_start(x2t[:, i % 2, :], x2_tok[i + 2]).then_inc(yk_in[i % 2], 16)
            for i in range(2):
                sp.wait_ge(out_done[i], 16 * (TT // 2))

        @block.gpsimd
        def _(pool):
            step = Steps(pool, pool_step)
            g = nc.gpsimd
            g.memset(ident[:, :], 0.0).then_inc(consts, 1)
            g.memset(ones[:, :], 1.0).then_inc(consts, 1)
            g.memset(eps[:, :], EPS).then_inc(consts, 1)
            g.iota(iota_f[:, :], pattern=[[1, P]], base=0, channel_multiplier=0,
                   allow_small_or_imprecise_dtypes=True).then_inc(consts, 1)
            g.memset(acc[0][:, :], 0.0).then_inc(acc_zero, 1)
            pool.wait_ge(acc_zero, 1)
            pool.dma_start(acc[0][0:1, :], a["b_ada"][0:1, 0:CH]).then_inc(acc_in[0], 16)
            pool.wait_ge(consts, 4)
            g.affine_select(out=ident[:, :], in_=ident[:, :], compare_op=ALU.not_equal, fill=1.0, base=0,
                            pattern=[[-1, P]], channel_multiplier=1).then_inc(consts, 1)
            g.iota(asgv[:, :, :], pattern=[[1, TOPK], [P * TOPK, TT]], base=1, channel_multiplier=TOPK,
                   allow_small_or_imprecise_dtypes=True).then_inc(consts, 1)
            g.affine_select(out=before[:, :], in_=ones[:, :], compare_op=ALU.is_gt, fill=0.0, base=0,
                            pattern=[[1, P]], channel_multiplier=-1).then_inc(consts, 1)
            pool.wait_ge(hT_done, KT)
            g.memset(gw[:, :, :, :], 0.0).then_inc(gw_zero, 1)
            g.memset(xrp[:, 0:CONV - 1], 0.0).then_inc(gw_zero, 1)
            pool.wait_ge(mod_done, 1)
            g.memset(acc[1][:, :], 0.0).then_inc(acc_zero, 1)
            pool.wait_ge(acc_zero, 2)
            pool.dma_start(acc[1][0:1, :], a["b_ada"][0:1, CH:2 * CH]).then_inc(acc_in[1], 16)
            pool.wait_ge(gates_ps, MT)
            g.memset(acc[2][:, :], 0.0).then_inc(acc_zero, 1)
            pool.wait_ge(acc_zero, 3)
            pool.dma_start(acc[2][0:1, :], a["b_ada"][0:1, 2 * CH:3 * CH]).then_inc(acc_in[2], 16)
            pool.wait_ge(chunk_used, W_KV)
            g.memset(qbd[:, :, :, :, :], 0.0).then_inc(qbd_zero, 1)

            pool.wait_ge(tab_done, 1)
            for i in range(TT):
                pool.wait_ge(h2_out[i], 16)
            g.memset(xg[:, :], 0.0).then_inc(xg_zero, 1)
            g.memset(small[:, 60:61], 0.0).then_inc(ysb_free, 1)
            pool.wait_ge(xg_zero, 1)

            def gather(at):
                g.tensor_copy(idx_now[:, 0:1], tok_i[:, at:at + 1]).then_inc(idx_done, 1)

            def gather_dma():
                pool.indirect_dma_start(out=xg[:, :], out_offset=None, in_=h2_d[:, :],
                                        in_offset=bass.IndirectOffsetOnAxis(ap=idx_now[:, 0:1].bitcast(U32), axis=0),
                                        bounds_check=SEQ - 1, oob_is_err=False).then_inc(xg_in, 16)

            def scatter_dma():
                pool.indirect_dma_start(out=yk_d[:, :], out_offset=bass.IndirectOffsetOnAxis(
                    ap=idx_now[:, 1:2].bitcast(U32), axis=0), in_=ysb[:, :], in_offset=None,
                                        bounds_check=SEQ * TOPK - 1, oob_is_err=False).then_inc(y_out, 16)

            gather(0)
            pool.wait_ge(idx_done, 1)
            gather_dma()

            def tick(n):
                return g.tensor_tensor(ticks[:, n:n + 1], eps[:, :], eps[:, :], ALU.add)

            def iteration(b):
                pool.wait_ge(xT_ps, b * 2 + 2)
                pool.wait_ge(xg_in, b * 16 + 16)
                g.tensor_copy(idx_now[:, 0:1], tok_i[:, bass.DynSlice(b + 1, 1)]).then_inc(idx_done, 1)
                pool.wait_ge(idx_done, b * 2 + 2)
                tick(0)
                gather_dma()
                g.tensor_copy(idx_now[:, 1:2], asg_i[:, bass.DynSlice(b, 1)]).then_inc(idx_done, 1)
                pool.wait_ge(idx_done, b * 2 + 3)
                pool.wait_ge(y_done, b + 2)
                tick(1)
                scatter_dma()
                pool.wait_ge(y_out, b * 16 + 16)
                tick(2).then_inc(ysb_free, 1)

            with pool.Fori(0, N_FIRST) as b:
                iteration(b)
            n_last = pool.value_load(over_i[0:1, N_LAST + 1:N_LAST + 2], min_val=1, max_val=N_LAST)
            with pool.Fori(0, N_LAST) as t:
                with pool.If(n_last > t):
                    iteration(t + N_FIRST)
            g.memset(small[:, 60:61], 0.0).then_inc(moe_done, 1)

        @block.scalar
        def _(act):
            step = Steps(act, act_step)
            s = nc.scalar

            act.dma_start(rows[R_C:R_C + KT, :], a["c"].rearrange("o (r c) -> (o r) c", c=P)).then_inc(rows_in, 16)
            for r0, name, sz in ((R_BMG, "b_merge_gate", 16), (R_GPM, "g_pre_mix", 8),
                                 (R_CONVB, "conv_b", MT), (R_LAM, "rg_lambda", MT)):
                act.dma_start(rows[r0:r0 + sz, :], a[name].rearrange("o (r c) -> (o r) c", c=P)).then_inc(rows_in, 16)
            act.dma_start(rows[R_CONVW:R_CONVW + CONV * MT, :], a["conv_w"][0].rearrange("j (r c) -> (j r) c", c=P)).then_inc(rows_in, 16)
            for r0, name in ((R_BA, "b_rg_a"), (R_BX, "b_rg_x")):
                act.dma_start(rows[r0:r0 + MT, :], a[name][0].rearrange("b j -> (b j)").rearrange("(r c) -> r c", c=P)).then_inc(rows_in, 16)
            act.dma_start(xt[:, :, :], x_tok).then_inc(x_in, 16)
            act.dma_start(gate_m[:, :], a["g_post_mix"].to_broadcast([P, D])).then_inc(gpost_in, 16)
            act.dma_start(gate_f[:, :], a["g_post_ffn"].to_broadcast([P, D])).then_inc(gpost_in, 16)
            sk = a["sinks"].rearrange("o (t h) -> h o t", h=2)
            for h in range(2):
                act.dma_start(sink[64 * h:64 * h + 64, :], sk[h].to_broadcast([64, 8]), allow_slow_non_contiguous=True).then_inc(small_in, 16)

            act.dma_start(freq[:, :], a["inv_freq"][:, :]).then_inc(small_in, 16)

            act.wait_ge(cols_done, 1)
            s.activation(small[:, 0:8], cols[:, R_C:R_C + 8], ACT.Exp, scale=-1.0).then_inc(cexp, 1)
            act.wait_ge(sp_exp, 1)
            s.activation(small[:, 20:30], small[:, 10:20], ACT.Exp, scale=-1.0).then_inc(cexp, 1)
            act.wait_ge(x_in, 16)
            for i in range(TT):
                if i:
                    act.wait_ge(ssq_done, i)
                s.activation(xjunk[:, :], xt[:, i, :], ACT.Square, accum_out=ssq[:, 0, i:i + 1]).then_inc(ssq_done, 1)
            act.wait_ge(ssq_done, TT)
            act.wait_ge(consts, 4)
            s.activation(ssq[:, 1, :], ssq[:, 0, :], ACT.Sqrt, bias=eps[:, 0:1], scale=1.0 / D).then_inc(rms_done, 1)
            for k in range(KT):
                act.wait_ge(htmp_done, k + 1)
                s.activation(hT[0][:, k, :], htmp[:, k % 2, :], ACT.Copy).then_inc(hT_hi, 1)

            def round_hi(w):
                if w >= W_MIX:
                    return
                n = WEIGHTS[w]
                c = words(STREAM[n])
                act.wait_ge(chunk_in[n % RS], 16 * (n // RS + 1))
                if w >= HS:
                    act.wait_ge(chunk_used, w - HS + 1)
                s.activation(hi[hi_slot(w)][:, 0:c], raw[n % RS][:, 0:c], ACT.Copy).then_inc(hi_done, 1)

            act.wait_ge(gw_zero, 1)
            for which, name in enumerate(("w_rg_a", "w_rg_x")):
                for q, b, r0, r1, c0, c1 in GATE_PIECES:
                    k, m = PAIRS[q]
                    act.dma_start(gw[r0 - k * P:r1 - k * P, which, q, c0 - m * P:c1 - m * P],
                                  a[name][0, b, r0 - b * RB:r1 - b * RB, c0 - b * RB:c1 - b * RB]).then_inc(gw_in, 16)

            round_hi(0)
            round_hi(1)
            act.wait_ge(sp_done, 1)
            for j in range(MT // 2):
                round_hi(2 * j + 2)
                for m in (2 * j, 2 * j + 1):
                    tile_ready(act, x_ps, m, 2 * j)
                    if m:
                        act.wait_ge(conv_done, m)
                    s.activation(xrp[:, CONV - 1:CONV - 1 + SEQ], ps[:, m % 2, :], ACT.Copy).then_inc(xrp_done, 1)
                round_hi(2 * j + 3)
                for m in READY[j]:
                    act.wait_ge(gates_ps, m + 1)
                    if m:
                        act.wait_ge(rnn_lo, m)
                    s.activation(th_a[:, :], ps[:, 2, :], ACT.Tanh, bias=bcol[:, 16 + m:17 + m], scale=0.5).then_inc(gates_read, 1)
                    s.activation(th_i[:, :], ps[:, 3, :], ACT.Tanh, bias=bcol[:, 26 + m:27 + m], scale=0.5).then_inc(gates_read, 1)
                    act.wait_ge(gates_read, 2 * m + 1)
                    s.activation(dec[:, :], th_a[:, :], ACT.Exp, bias=sp4[:, 1, m:m + 1], scale=sp4[:, 1, m:m + 1]).then_inc(a_done, 1)
                    s.activation(t_om[:, :], th_a[:, :], ACT.Tanh, bias=sp4[:, 0, m:m + 1], scale=sp4[:, 0, m:m + 1]).then_inc(a_done, 1)
                    act.wait_ge(a_done, 3 * m + 1)
                    s.activation(sq[:, :], dec[:, :], ACT.Square).then_inc(a_done, 1)
                    tile_ready(act, g_ps, m, 2 * (m // 2) + 1)
                    s.activation(gr[:, :], ps[:, 4 + m % 4, :], ACT.Copy).then_inc(g2_done, 1)
                    s.activation(g2[:, :], ps[:, 4 + m % 4, :], ACT.Square).then_inc(g2_done, 1)
                    act.wait_ge(inner_done, m + 1)
                    s.activation(g2[:, :], g2[:, :], ACT.Tanh, scale=0.7978845608028654).then_inc(gelu_th, 1)
                    act.wait_ge(om_done, m + 1)
                    s.activation(sq[:, :], sq[:, :], ACT.Sqrt).then_inc(sqrt_done, 1)
                    act.wait_ge(rnn_done, m + 1)
                    s.activation(rnnT[0][:, m, :], g2[:, :], ACT.Copy).then_inc(rnn_hi, 1)

            act.wait_ge(rnn_lo, MT)
            act.dma_start(scale_f[:, :], a["g_pre_ffn"].to_broadcast([P, D])).then_inc(gpost_in, 16)
            for p in range(4):
                w = W_BR + 3 * p
                round_hi(w + 2)
                for t in (2 * p, 2 * p + 1):
                    tile_ready(act, bg_ps, t, w)
                    if t >= 2:
                        act.wait_ge(bm_done, t - 1)
                    s.activation(gate_s[:, t % 2, :], ps[:, 4 * (p % 2) + t % 2, :], ACT.Tanh,
                                 bias=bcol[:, 8 + t:9 + t], scale=0.5).then_inc(bg_done, 1)
                round_hi(w + 3)
                round_hi(w + 4)

            act.wait_ge(bm_done, KT)
            act.dma_start(kpos[:, :], a["positions"].to_broadcast([P, SEQ])).then_inc(pos_in, 16)
            act.wait_ge(ang_done, 1)
            s.activation(cos[:, :], cos[:, :], ACT.Sin).then_inc(trig_done, 1)
            act.wait_ge(ang_done, 2)
            s.activation(sin[:, :], sin[:, :], ACT.Sin).then_inc(trig_done, 1)

            def swap_halves(bank):
                for q in range(4):
                    last = s.activation(swp[32 * q:32 * q + 32, :], ps[32 * (q ^ 1):32 * (q ^ 1) + 32, bank, :], ACT.Copy)
                last.then_inc(swp_done, 1)

            act.wait_ge(kv_ps, 1)
            swap_halves(0)
            act.wait_ge(rope_done, 1)
            for g_ in range(NKV):
                for h in range(2):
                    s.activation(kT[64 * h:64 * h + 64, g_, :], rot[64 * g_:64 * g_ + 64, :], ACT.Copy).then_inc(kT_done, 1)
            act.wait_ge(chunk_used, W_KV + 1)
            for twice in range(2):
                for bank, b0, nb in ((1, 0, 4), (2, 4, 3)):
                    s.activation(vb[:, b0:b0 + nb, :, twice, :],
                                 ps[:, bank, 0:nb * P].rearrange("p (b g d) -> p b g d", g=NKV, d=HD), ACT.Copy).then_inc(v_done, 1)
            round_hi(W_Q + 1)
            for g_ in range(NKV):
                round_hi(W_Q + 2 * g_ + 2)
                round_hi(W_Q + 2 * g_ + 3)
                for t in range(4 * g_, 4 * g_ + 4):
                    tile_ready(act, q_ps, t, W_Q + t // 2)
                    act.wait_ge(rope_done, t + 1)
                    swap_halves(4 + t % 4)
                for c in range(NC + 1):
                    if c < NC:
                        u = NC * g_ + c
                        n = CHUNK if c == 0 else 2 * CHUNK
                        act.wait_ge(m_done, u + 1)
                        for jj in range(4):
                            ins = s.activation(prob[:, u % 2, jj, 0:n], ps[:, u % 2, jj * P:jj * P + n], ACT.Exp,
                                               bias=small[:, 8 * (u % 2) + jj:8 * (u % 2) + jj + 1], scale=HD ** -0.5,
                                               accum_out=small[:, 16 + 8 * (u % 2) + jj:17 + 8 * (u % 2) + jj])
                        ins = s.activation(small[:, 32 + 8 * (u % 2):36 + 8 * (u % 2)], small[:, 4 + 8 * (u % 2):8 + 8 * (u % 2)], ACT.Exp)
                        ins.then_inc(e_done, 1)
                    if c:
                        u = NC * g_ + c - 1
                        n = CHUNK if c == 1 else 2 * CHUNK
                        act.wait_ge(pT_ps, u + 1)
                        if u >= 2:
                            act.wait_ge(o_ps, u - 1)
                        s.activation(probT[0:n, u % 2, :, :], ps[0:n, 2 + u % 2, :].rearrange("p (j n) -> p j n", n=P), ACT.Copy).then_inc(pT_done, 1)
                        act.wait_ge(o_ps, u + 1)
                        for h in range(2):
                            s.activation(attnT[0][64 * h:64 * h + 64, 4 * g_:4 * g_ + 4, CHUNK * (c - 1):CHUNK * c],
                                         ps[64 * h:64 * h + 64, 4 + u % 2, :].rearrange("p (j h q) -> p j h q", h=2, q=CHUNK)[:, :, h, :],
                                         ACT.Copy).then_inc(o_hi, 1)

            for p in range(4):
                w = W_BA + 2 * p
                round_hi(w + 2)
                for t in (2 * p, 2 * p + 1):
                    tile_ready(act, ag_ps, t, w)
                    if t >= 2:
                        act.wait_ge(mrg_sum, t - 1)
                    s.activation(gate_a[:, t % 2, :], ps[:, 4 * (p % 2) + t % 2, :], ACT.Tanh,
                                 bias=bcol[:, t:t + 1], scale=0.5).then_inc(bg_done, 1)
                round_hi(w + 3)
                for t in (2 * p, 2 * p + 1):
                    act.wait_ge(mrg_sum, t + 1)
                    s.activation(mrgT[0][:, t, :], mtmp[:, t % 2, :], ACT.Copy, scale=0.5).then_inc(mrg_hi, 1)

            round_hi(W_OUT + 2)
            round_hi(W_OUT + 3)
            act.wait_ge(mrg_done, KT)
            act.dma_start(x2[:, :, :], x_tok).then_inc(xe_in, 16)
            act.dma_start(btab[:, 0:2 * DE], a["b_e1"][0]).then_inc(bt_in, 16)
            act.dma_start(btab[:, 2 * DE:3 * DE], a["b_e2"][0]).then_inc(bt_in, 16)
            act.dma_start(wr[:, :, :], a["w_router"][0].rearrange("(k p) n -> p k n", p=P)).then_inc(bt_in, 16)
            act.dma_start(brt[:, :], a["b_router"].to_broadcast([P, NE])).then_inc(bt_in, 16)
            act.wait_ge(bpart_done, 1)
            act.wait_ge(chunk_used, W_MIX)
            for i in range(TT):
                if i:
                    act.wait_ge(e_ssq, i)
                s.activation(junk[:, :].rearrange("p (b n) -> p b n", b=2), ps[:, 2 * i:2 * i + 2, :], ACT.Square,
                             accum_out=ssq[:, 0, i:i + 1]).then_inc(e_ssq, 1)
            act.wait_ge(e_ssq, TT)
            s.activation(ssq[:, 1, :], ssq[:, 0, :], ACT.Sqrt, bias=eps[:, 0:1], scale=1.0 / D).then_inc(e_rms, 1)
            for i in range(TT):
                act.wait_ge(x2_done, i + 1)
                act.wait_ge(e_ssq, TT + i)
                s.activation(junk[:, :], x2[:, i, :], ACT.Square, accum_out=ssq[:, 2, i:i + 1]).then_inc(e_ssq, 1)
            act.wait_ge(e_ssq, 2 * TT)
            s.activation(ssq[:, 3, :], ssq[:, 2, :], ACT.Sqrt, bias=eps[:, 0:1], scale=1.0 / D).then_inc(e_rms, 1)
            act.dma_start(x2_d.rearrange("(i p) d -> p i d", p=P), x2[:, :, :]).then_inc(x2_out, 16)
            for i in range(TT):
                act.wait_ge(h2_done, i + 1)
                act.dma_start(h2_d[i * P:(i + 1) * P, :], h2[:, i % 2, :]).then_inc(h2_out[i], 16)
                act.wait_ge(h2_tr, i + 1)
                if i:
                    act.wait_ge(lg_ps, i)
                s.activation(hfT[:, :, :], ps[:, 2 * i:2 * i + 2, :].rearrange("p b (k n) -> p (b k) n", n=P), ACT.Copy).then_inc(hfT_done, 1)
            act.wait_ge(wsub, 1)
            for i in range(TT):
                s.activation(topw[:, i, :], topw[:, i, :], ACT.Exp, accum_out=ssq[:, 0, i:i + 1]).then_inc(wexp, 1)

            def hi_x(b, half):
                act.wait_ge(xT_ps, b * 2 + (half + 1))
                s.activation(xT[0][:, 4 * half:4 * half + 4, :], ps[:, 6 + half, :].rearrange("p (k n) -> p k n", n=P), ACT.Copy).then_inc(xT_hi, 1)

            def hi_w(b, i):
                act.wait_ge(chunk_in[i], b * 16 + 16 * (mix_uses[i] + 1))
                act.wait_ge(chunk_used, b * MS + (W_MIX + i - HS + 1))
                s.activation(hi[i % HS][:, :], raw[i][:, :], ACT.Copy).then_inc(hi_done, 1)

            def sigmoid(b, half):
                act.wait_ge(chunk_used, b * MS + (W_MIX + 4 * half + 2))
                if half:
                    act.wait_ge(glu_done, b * 2 + 1)
                s.activation(sg[:, :], ps[:, 2 * half, :], ACT.Sigmoid, scale=ALPHA).then_inc(sg_done, 1)

            def hi_a(b, half):
                act.wait_ge(aT_ps, b * 2 + (half + 1))
                s.activation(aT[0][:, 4 * half:4 * half + 4, :], ps[:, 6 + half, :].rearrange("p (k n) -> p k n", n=P), ACT.Copy).then_inc(aT_hi, 1)

            def iteration(b, more):
                for i in range(3, MS):
                    hi_w(b, i)
                    if i == 5:
                        sigmoid(b, 0)
                    if i == 8:
                        hi_a(b, 0)
                    if i == 9:
                        sigmoid(b, 1)
                hi_x(b + 1, 0)
                more(lambda: hi_w(b + 1, 0))
                hi_a(b, 1)

                def two():
                    hi_w(b + 1, 1)
                    hi_w(b + 1, 2)
                more(two)
                hi_x(b + 1, 1)
                act.wait_ge(ysb_free, b + 1)
                act.wait_ge(chunk_used, b * MS + (W_MIX + MS))
                s.activation(ysb[:, :].rearrange("p (h n) -> p h n", h=2), ps[:, 4:6, :], ACT.Copy).then_inc(y_done, 1)

            s.activation(small[:, 61:62], eps[:, :], ACT.Copy).then_inc(y_done, 1)
            for i in range(3):
                hi_w(0, i)
            hi_x(0, 0)
            hi_x(0, 1)
            with act.Fori(0, N_FIRST) as b:
                iteration(b, lambda f: f())
            n_last = act.value_load(over_i[0:1, N_LAST + 1:N_LAST + 2], min_val=1, max_val=N_LAST)
            with act.Fori(0, N_LAST) as t:
                with act.If(n_last > t):
                    def if_more(f):
                        with act.If(n_last > t + 1):
                            f()
                    iteration(t + N_FIRST, if_more)
            for i in range(TT):
                act.wait_ge(comb_done, i + 1)
                s.activation(tjunk[:, :], comb[:, i % 2, :], ACT.Square, accum_out=ssq[:, 0, i:i + 1]).then_inc(t_ssq, 1)
                act.wait_ge(t_ssq, 2 * i + 1)
                s.activation(ssq[:, 1, i:i + 1], ssq[:, 0, i:i + 1], ACT.Sqrt, bias=eps[:, 0:1], scale=1.0 / D).then_inc(t_ssq, 1)

        @block.vector
        def _(dve):
            v = nc.vector
            step = Steps(dve, dve_step)
            link = step.link
            done_items = [0]

            def col(r):
                return cols[:, r:r + 1]

            def advance(w):
                while w < W_MIX and done_items[0] <= WEIGHTS[w]:
                    n = done_items[0]
                    done_items[0] += 1
                    it, r = STREAM[n], raw[n % RS]
                    if it[0] == "ada":
                        q = ADAS.index(n)
                        part, k = it[1], it[2]
                        dve.wait_ge(chunk_in[n % RS], 16 * (n // RS + 1))
                        if k == 0:
                            dve.wait_ge(acc_in[part], 16)
                        else:
                            dve.wait_ge(ada_used, q)
                        v.scalar_tensor_tensor(out=acc[part][:, :], in0=r[:, :], scalar=scol[:, k:k + 1],
                                               in1=acc[part][:, :], op0=ALU.mult, op1=ALU.add).then_inc(ada_used, 1)
                    else:
                        ww = WEIGHTS.index(n)
                        c = words(it)
                        dve.wait_ge(hi_done, ww + 1)
                        v.tensor_tensor(lo[n % RS][:, 0:c], r[:, 0:c], hi[hi_slot(ww)][:, 0:c].bitcast(F32),
                                        ALU.subtract).then_inc(split_done, 1)

            dve.wait_ge(cols_ps, 1)
            v.tensor_copy(cols[:, :], ps[:, 7, 0:R_END]).then_inc(cols_done, 1)
            dve.wait_ge(cols_done, 1)
            dve.wait_ge(cexp, 1)
            link(v.tensor_scalar(small[:, 0:8], small[:, 0:8], 1.0, None, ALU.add))
            link(v.reciprocal(small[:, 0:8], small[:, 0:8]))
            v.tensor_tensor(scol[:, :], cols[:, R_C:R_C + 8], small[:, 0:8], ALU.mult).then_inc(scol_done, 1)
            link(v.tensor_scalar(small[:, 30:40], cols[:, R_LAM:R_LAM + MT], -1.0, None, ALU.mult))
            v.tensor_tensor(small[:, 10:20], small[:, 30:40], cols[:, R_LAM:R_LAM + MT], ALU.max).then_inc(sp_exp, 1)
            link(v.tensor_scalar(small[:, 30:40], small[:, 30:40], 0.0, None, ALU.max))
            v.tensor_scalar(bcol[:, 0:16], cols[:, R_BMG:R_BMG + 16], 0.5, None, ALU.mult)
            v.tensor_scalar(bcol[:, 16:26], cols[:, R_BA:R_BA + MT], 0.5, None, ALU.mult)
            link(v.tensor_scalar(bcol[:, 26:36], cols[:, R_BX:R_BX + MT], 0.5, None, ALU.mult))
            dve.wait_ge(cexp, 2)
            e_, z_, z2_, p_ = small[:, 20:30], small[:, 40:50], small[:, 50:60], small[:, 10:20]
            link(v.tensor_scalar(z_, e_, 2.0, None, ALU.add))
            link(v.reciprocal(z_, z_))
            link(v.tensor_tensor(z_, z_, e_, ALU.mult))
            link(v.tensor_tensor(z2_, z_, z_, ALU.mult))
            link(v.tensor_scalar(p_, z2_, 1.0 / 17, 1.0 / 15, ALU.mult, ALU.add))
            for t in (13, 11, 9, 7, 5, 3, 1):
                link(v.tensor_tensor(p_, p_, z2_, ALU.mult))
                link(v.tensor_scalar(p_, p_, 1.0 / t, None, ALU.add))
            link(v.tensor_tensor(p_, p_, z_, ALU.mult))
            link(v.scalar_tensor_tensor(out=p_, in0=p_, scalar=2.0, in1=small[:, 30:40], op0=ALU.mult, op1=ALU.add))
            v.tensor_scalar(sp4[:, 0, :], p_, 4.0, None, ALU.mult)
            v.tensor_scalar(sp4[:, 1, :], p_, -4.0, None, ALU.mult).then_inc(sp_done, 1)
            dve.wait_ge(rms_done, 1)
            link(v.reciprocal(ssq[:, 1, :], ssq[:, 1, :]))
            for i in range(TT):
                v.tensor_scalar(xt[:, i, :], xt[:, i, :], ssq[:, 1, i:i + 1], None, ALU.mult).then_inc(xn_done, 1)
            dve.wait_ge(scol_done, 1)
            while STREAM[done_items[0]][0] == "ada":
                n = done_items[0]
                done_items[0] += 1
                k = STREAM[n][2]
                dve.wait_ge(chunk_in[n % RS], 16 * (n // RS + 1))
                if k == 0:
                    dve.wait_ge(acc_in[0], 16)
                else:
                    dve.wait_ge(ada_used, k)
                v.scalar_tensor_tensor(out=acc[0][:, :], in0=raw[n % RS][:, :], scalar=scol[:, k:k + 1],
                                       in1=acc[0][:, :], op0=ALU.mult, op1=ALU.add).then_inc(ada_used, 1)
            dve.wait_ge(mod_ps, 1)
            link(v.tensor_copy(modc[:, 0, :], ps[:, 6, 0:KT]))
            link(v.tensor_scalar(modc[:, 1, :], ps[:, 6, KT:2 * KT], 1.0, None, ALU.add))
            v.tensor_tensor(modc[:, 1, :], modc[:, 1, :], cols[:, R_GPM:R_GPM + KT], ALU.mult).then_inc(mod_done, 1)
            dve.wait_ge(mod_done, 1)
            for k in range(KT + 1):
                if k < KT:
                    dve.wait_ge(tr_done, k + 1)
                    if k >= 2:
                        dve.wait_ge(hT_hi, k - 1)
                        dve.wait_ge(hT_done, k - 1)
                    v.tensor_scalar(htmp[:, k % 2, :], ps[:, k % 4, :], modc[:, 1, k:k + 1], modc[:, 0, k:k + 1],
                                    ALU.mult, ALU.add).then_inc(htmp_done, 1)
                if k:
                    dve.wait_ge(htmp_done, k)
                    dve.wait_ge(hT_hi, k)
                    ins = v.tensor_tensor(hT[1][:, k - 1, :], htmp[:, (k - 1) % 2, :], hT[0][:, k - 1, :].bitcast(F32), ALU.subtract)
                    ins.then_inc(hT_done, 1)

            advance(1)
            for j in range(MT // 2):
                advance(2 * j + 2)
                for m in (2 * j, 2 * j + 1):
                    if m == 0:
                        dve.wait_ge(gw_zero, 2)
                    dve.wait_ge(xrp_done, m + 1)
                    x_, w_ = xc[:, m % 4, :], [col(R_CONVW + t * MT + m) for t in range(CONV)]
                    link(v.tensor_scalar(x_, xrp[:, 0:SEQ], w_[0], col(R_CONVB + m), ALU.mult, ALU.add))
                    for t in range(1, CONV):
                        ins = v.scalar_tensor_tensor(out=x_, in0=xrp[:, t:t + SEQ], scalar=w_[t], in1=x_, op0=ALU.mult, op1=ALU.add)
                        if t < CONV - 1:
                            link(ins)
                    ins.then_inc(conv_done, 1)
                advance(2 * j + 3)
                for m in READY[j]:
                    dve.wait_ge(g2_done, 2 * m + 2)
                    link(v.scalar_tensor_tensor(out=g2[:, :], in0=g2[:, :], scalar=0.044715, in1=gr[:, :], op0=ALU.mult, op1=ALU.mult))
                    v.tensor_tensor(g2[:, :], g2[:, :], gr[:, :], ALU.add).then_inc(inner_done, 1)
                    dve.wait_ge(a_done, 3 * m + 3)
                    v.scalar_tensor_tensor(out=sq[:, :], in0=sq[:, :], scalar=1.0, in1=t_om[:, :], op0=ALU.add, op1=ALU.mult).then_inc(om_done, 1)
                    dve.wait_ge(gates_read, 2 * m + 2)
                    dve.wait_ge(conv_done, m + 1)
                    link(v.scalar_tensor_tensor(out=th_i[:, :], in0=th_i[:, :], scalar=1.0, in1=xc[:, m % 4, :], op0=ALU.add, op1=ALU.mult))
                    dve.wait_ge(gelu_th, m + 1)
                    link(v.scalar_tensor_tensor(out=g2[:, :], in0=g2[:, :], scalar=1.0, in1=gr[:, :], op0=ALU.add, op1=ALU.mult))
                    dve.wait_ge(sqrt_done, m + 1)
                    link(v.scalar_tensor_tensor(out=th_i[:, :], in0=th_i[:, :], scalar=0.5, in1=sq[:, :], op0=ALU.mult, op1=ALU.mult))
                    link(v.tensor_tensor_scan(out=th_a[:, :], data0=dec[:, :], data1=th_i[:, :], initial=0.0, op0=ALU.mult, op1=ALU.add))
                    v.scalar_tensor_tensor(out=g2[:, :], in0=g2[:, :], scalar=0.5, in1=th_a[:, :], op0=ALU.mult, op1=ALU.mult).then_inc(rnn_done, 1)
                    dve.wait_ge(rnn_done, m + 1)
                    dve.wait_ge(rnn_hi, m + 1)
                    v.tensor_tensor(rnnT[1][:, m, :], g2[:, :], rnnT[0][:, m, :].bitcast(F32), ALU.subtract).then_inc(rnn_lo, 1)

            dve.wait_ge(gpost_in, 48)
            for p in range(4):
                w = W_BR + 3 * p
                advance(w + 2)
                advance(w + 3)
                for t in (2 * p, 2 * p + 1):
                    dve.wait_ge(bg_done, t + 1)
                    tile_ready(dve, bp_ps, t, w + 2)
                    v.scalar_tensor_tensor(out=mix[:, t, :], in0=gate_s[:, t % 2, :], scalar=1.0,
                                           in1=ps[:, 4 * (p % 2) + 2 + t % 2, :], op0=ALU.add, op1=ALU.mult).then_inc(bm_done, 1)
                if p == 0:
                    for q in range(4):
                        dve.wait_ge(mod_ps, 2 + q)
                        h = slice(512 * (q % 2), 512 * (q % 2) + 512)
                        if q < 2:
                            ins = v.tensor_tensor(gate_m[:, h], gate_m[:, h], ps[:, 4 + q, :], ALU.mult)
                        else:
                            ins = v.tensor_copy(shift_f[:, h], ps[:, 4 + q, :])
                        ins.then_inc(mod_done, 1)
                advance(w + 4)
            for q in range(4):
                dve.wait_ge(mod_ps, 6 + q)
                h = slice(512 * (q % 2), 512 * (q % 2) + 512)
                if q < 2:
                    ins = v.scalar_tensor_tensor(out=scale_f[:, h], in0=ps[:, q, :], scalar=1.0, in1=scale_f[:, h], op0=ALU.add, op1=ALU.mult)
                else:
                    ins = v.tensor_tensor(gate_f[:, h], gate_f[:, h], ps[:, q, :], ALU.mult)
                ins.then_inc(mod_done, 1)

            advance(W_KV + 1)
            dve.wait_ge(pos_in, 16)
            dve.wait_ge(small_in, 48)
            dve.wait_ge(mod_done, 9)
            ang, turns = prob[:, 0, :, :].rearrange("p a b -> p (a b)"), prob[:, 1, :, :].rearrange("p a b -> p (a b)")
            link(v.tensor_copy(ang, kpos[:, :]))
            link(v.tensor_scalar(ang, ang, freq[:, 0:1], None, ALU.mult))
            MAGIC, C1 = 12582912.0, 6.28125
            C2, C3 = 0.0019350051879882812, 3.0199157663854277e-07
            for r, quarter in ((cos, 0.25), (sin, 0.0)):
                link(v.tensor_scalar(turns, ang, 0.15915494309189535, quarter, ALU.mult, ALU.add))
                link(v.tensor_scalar(turns, turns, MAGIC, None, ALU.add))
                link(v.tensor_scalar(turns, turns, MAGIC, None, ALU.subtract))
                link(v.scalar_tensor_tensor(out=r[:, :], in0=turns, scalar=-C1, in1=ang, op0=ALU.mult, op1=ALU.add))
                link(v.scalar_tensor_tensor(out=r[:, :], in0=turns, scalar=-C2, in1=r[:, :], op0=ALU.mult, op1=ALU.add))
                link(v.scalar_tensor_tensor(out=r[:, :], in0=turns, scalar=-C3, in1=r[:, :], op0=ALU.mult, op1=ALU.add))
                if quarter:
                    link(v.tensor_scalar(r[:, :], r[:, :], 1.5707963267948966, None, ALU.add))
                v.tensor_scalar(r[:, :], r[:, :], 3.1415925, -3.1415925, ALU.min, ALU.max).then_inc(ang_done, 1)
            dve.wait_ge(trig_done, 2)
            for h in range(2):
                ins = v.tensor_scalar(sin[64 * h:64 * h + 32, :], sin[64 * h:64 * h + 32, :], -1.0, None, ALU.mult)
            link(ins)

            def rotate(bank):
                v.tensor_tensor(rot[:, :], ps[:, bank, :], cos[:, :], ALU.mult)
                link(v.tensor_tensor(swp[:, :], swp[:, :], sin[:, :], ALU.mult))

            dve.wait_ge(kv_ps, 1)
            dve.wait_ge(swp_done, 1)
            rotate(0)
            v.tensor_tensor(rot[:, :], rot[:, :], swp[:, :], ALU.add).then_inc(rope_done, 1)
            advance(W_Q + 1)
            for g_ in range(NKV):
                advance(W_Q + 2 * g_ + 2)
                for t in range(4 * g_, 4 * g_ + 4):
                    if t % 4 == 2:
                        advance(W_Q + 2 * g_ + 3)
                    if t == 0:
                        dve.wait_ge(kT_done, 4)
                        dve.wait_ge(qbd_zero, 1)
                    if t == 4:
                        dve.wait_ge(s_ps, NC)
                    tile_ready(dve, q_ps, t, W_Q + t // 2)
                    dve.wait_ge(swp_done, t + 2)
                    dve.wait_ge(rope_done, t + 1)
                    rotate(4 + t % 4)
                    for h in range(2):
                        hs = slice(64 * h, 64 * h + 64)
                        ins = v.tensor_tensor(qbd[hs, t % 4, :, h, :], rot[hs, :].rearrange("p (c q) -> p c q", q=CHUNK),
                                              swp[hs, :].rearrange("p (c q) -> p c q", q=CHUNK), ALU.add)
                    ins.then_inc(rope_done, 1)
                for c in range(NC + 1):
                    if c < NC:
                        u = NC * g_ + c
                        n = CHUNK if c == 0 else 2 * CHUNK
                        o = 8 * (u % 2)
                        dve.wait_ge(s_ps, u + 1)
                        if u >= 2:
                            dve.wait_ge(e_done, u - 1)
                        if u:
                            dve.wait_ge(p_done, u)
                        link(v.tensor_reduce(small[:, 48:52], ps[:, u % 2, :].rearrange("p (j n) -> p j n", n=P)[:, :, 0:n], AX_X, ALU.max))
                        link(v.scalar_tensor_tensor(out=small[:, 48:52], in0=small[:, 48:52], scalar=HD ** -0.5,
                                                    in1=sink[:, 4 * g_:4 * g_ + 4], op0=ALU.mult, op1=ALU.max))
                        v.tensor_scalar(small[:, o:o + 4], small[:, 48:52], -1.0, None, ALU.mult)
                        v.tensor_tensor(small[:, o + 4:o + 8], sink[:, 4 * g_:4 * g_ + 4], small[:, 48:52], ALU.subtract).then_inc(m_done, 1)
                        dve.wait_ge(e_done, u + 1)
                        link(v.tensor_tensor(small[:, 52:56], small[:, 16 + o:20 + o], small[:, 32 + o:36 + o], ALU.add))
                        link(v.reciprocal(small[:, 52:56], small[:, 52:56]))
                        v.tensor_tensor(prob[:, u % 2, :, 0:n], prob[:, u % 2, :, 0:n],
                                        small[:, 52:56].unsqueeze(2).to_broadcast([P, 4, n]), ALU.mult).then_inc(p_done, 1)
                    if c:
                        u = NC * g_ + c - 1
                        dve.wait_ge(o_hi, 2 * u + 2)
                        for h in range(2):
                            hs, cs = slice(64 * h, 64 * h + 64), slice(CHUNK * (c - 1), CHUNK * c)
                            ins = v.tensor_tensor(attnT[1][hs, 4 * g_:4 * g_ + 4, cs],
                                                  ps[hs, 4 + u % 2, :].rearrange("p (j h q) -> p j h q", h=2, q=CHUNK)[:, :, h, :],
                                                  attnT[0][hs, 4 * g_:4 * g_ + 4, cs].bitcast(F32), ALU.subtract)
                        ins.then_inc(o_done, 1)

            for p in range(4):
                w = W_BA + 2 * p
                advance(w + 2)
                advance(w + 3)
                for t in (2 * p, 2 * p + 1):
                    dve.wait_ge(bg_done, KT + t + 1)
                    if t >= 2:
                        dve.wait_ge(mrg_done, t - 1)
                    tile_ready(dve, ap_ps, t, w + 1)
                    link(v.scalar_tensor_tensor(out=mtmp[:, t % 2, :], in0=gate_a[:, t % 2, :], scalar=1.0,
                                                in1=ps[:, 4 * (p % 2) + 2 + t % 2, :], op0=ALU.add, op1=ALU.mult))
                    v.tensor_tensor(mtmp[:, t % 2, :], mtmp[:, t % 2, :], mix[:, t, :], ALU.add).then_inc(mrg_sum, 1)
                    dve.wait_ge(mrg_hi, t + 1)
                    v.scalar_tensor_tensor(out=mrgT[1][:, t, :], in0=mtmp[:, t % 2, :], scalar=0.5,
                                           in1=mrgT[0][:, t, :].bitcast(F32), op0=ALU.mult, op1=ALU.subtract).then_inc(mrg_done, 1)
            advance(W_MIX - 1)

            dve.wait_ge(bt_in, 64)
            for part in range(3):
                link(v.tensor_copy(bt16[:, :], btab[:, :]))
                link(v.tensor_copy(bpart[NE * part:NE * part + NE, :], bt16[:, :]))
                if part < 2:
                    link(v.tensor_tensor(btab[:, :], btab[:, :], bt16[:, :], ALU.subtract))
            for part in range(3):
                q = slice(NE * part, NE * part + NE)
                link(v.tensor_copy(onehot[q, :], ident[q, q]))
            v.tensor_copy(sel[:, :], onehot[:, 0:1].to_broadcast([3 * NE, P])).then_inc(sel_done, 1)
            v.memset(over_f[:, :], float(NE - 1)).then_inc(bpart_done, 1)

            dve.wait_ge(e_rms, 1)
            dve.wait_ge(xe_in, 16)
            link(v.reciprocal(ssq[:, 1, :], ssq[:, 1, :]))
            for i in range(TT):
                if i:
                    dve.wait_ge(x2_done, i)
                link(v.scalar_tensor_tensor(out=h2[:, 0, :], in0=ps[:, 2 * i:2 * i + 2, :].rearrange("p b n -> p (b n)"),
                                            scalar=ssq[:, 1, i:i + 1], in1=gate_m[:, :], op0=ALU.mult, op1=ALU.mult))
                v.tensor_tensor(x2[:, i, :], x2[:, i, :], h2[:, 0, :], ALU.add).then_inc(x2_done, 1)
            dve.wait_ge(x2_done, TT)
            dve.wait_ge(e_rms, 2)
            link(v.reciprocal(ssq[:, 3, :], ssq[:, 3, :]))
            for i in range(TT):
                if i >= 2:
                    dve.wait_ge(h2_tr, i - 1)
                    dve.wait_ge(h2_out[i - 2], 16)
                link(v.scalar_tensor_tensor(out=h2[:, i % 2, :], in0=x2[:, i, :], scalar=ssq[:, 3, i:i + 1], in1=scale_f[:, :],
                                            op0=ALU.mult, op1=ALU.mult))
                v.tensor_tensor(h2[:, i % 2, :], h2[:, i % 2, :], shift_f[:, :], ALU.add).then_inc(h2_done, 1)

            lg, oh, prod = route[:, 0:TT, :], ohe[:, 0, :, :], ohe[:, 1, :, :]
            mask, q0, q1, blk = (route[:, 4 * t:4 * t + 4, :] for t in range(1, 5))
            cnt, nb, incl, basep = (route[:, 20 + t, :] for t in range(4))
            iota_e = iota_f[:, 0:NE]
            for i in range(TT):
                dve.wait_ge(lg_ps, i + 1)
                link(v.tensor_tensor(lg[:, i, :], ps[:, 2 * i, 0:NE], brt[:, :], ALU.add))
                link(v.max(top8[:, i, :], lg[:, i, :]))
                link(v.max_index(idx8[:, i, :], top8[:, i, :], lg[:, i, :]))
            link(v.tensor_copy(idxf[:, :, :], idx8[:, :, :]))
            for k in range(TOPK):
                for i in range(TT):
                    ins = v.tensor_scalar(oh[:, TT * k + i, :], iota_e, idxf[:, i, k:k + 1], None, ALU.is_equal)
            link(ins)
            link(v.tensor_tensor(mask, oh[:, 0:TT, :], oh[:, TT:2 * TT, :], ALU.add))
            link(v.tensor_tensor(mask, mask, oh[:, 2 * TT:3 * TT, :], ALU.add))
            v.tensor_tensor(mask, mask, oh[:, 3 * TT:4 * TT, :], ALU.add).then_inc(mask_done, 1)
            for i in range(TT):
                ins = v.tensor_scalar(topw[:, i, :], top8[:, i, 0:TOPK], top8[:, i, 0:1], None, ALU.subtract)
            ins.then_inc(wsub, 1)
            dve.wait_ge(rank_ps, 1)
            link(v.tensor_copy(cnt, ps[:, 1, 0:NE]))
            link(v.tensor_scalar(nb, cnt, float(P + 1), None, ALU.is_ge))
            for t in (2, 3):
                link(v.scalar_tensor_tensor(out=nb, in0=cnt, scalar=float(t * P + 1), in1=nb, op0=ALU.is_ge, op1=ALU.add))
            link(v.tensor_tensor_scan(out=incl, data0=ones[:, 0:NE], data1=nb, initial=0.0, op0=ALU.mult, op1=ALU.add))
            link(v.scalar_tensor_tensor(out=basep, in0=incl, scalar=float(NE - 1), in1=nb, op0=ALU.add, op1=ALU.subtract))
            link(v.tensor_tensor(basep, basep, iota_e, ALU.subtract))
            rank = ps[:, 0, 0:TT * NE].rearrange("p (i e) -> p i e", e=NE)
            link(v.tensor_scalar(q0, rank, float(P), None, ALU.is_ge))
            link(v.scalar_tensor_tensor(out=q1, in0=rank, scalar=float(2 * P), in1=q0, op0=ALU.is_ge, op1=ALU.add))
            link(v.scalar_tensor_tensor(out=q1, in0=rank, scalar=float(3 * P), in1=q1, op0=ALU.is_ge, op1=ALU.add))
            link(v.tensor_tensor(blk, q0, basep.unsqueeze(1).to_broadcast([P, TT, NE]), ALU.mult))
            link(v.tensor_tensor(blk, blk, iota_e.unsqueeze(1).to_broadcast([P, TT, NE]), ALU.add))
            link(v.tensor_tensor(blk, blk, q1, ALU.add))
            link(v.scalar_tensor_tensor(out=q0, in0=q1, scalar=-float(P), in1=rank, op0=ALU.mult, op1=ALU.add))
            for t, val in ((0, blk), (1, q0)):
                for k in range(TOPK):
                    ins = v.tensor_tensor(prod[:, TT * k:TT * k + TT, :], oh[:, TT * k:TT * k + TT, :], val, ALU.mult)
                link(ins)
                link(v.tensor_reduce(pick[:, t, :], prod, AX_X, ALU.add))
            dve.wait_ge(x2_out, 16)
            for q in range(TOPK * TT):
                v.tensor_scalar(oh_slot[:, q, :], iota_f[:, :], pick[:, 1, q:q + 1], None, ALU.is_equal)
                v.tensor_scalar(oh_blk[:, q, 0:N_BLOCKS + 1], iota_f[:, 0:N_BLOCKS + 1], pick[:, 0, q:q + 1],
                                asgv[:, q // TT, q % TT:q % TT + 1], ALU.is_equal, ALU.mult).then_inc(oh_done, 1)
            for o in range(N_OVER):
                ins = v.tensor_scalar(route[:, 24 + o, :], incl, float(o), None, ALU.is_le)
            link(ins)
            link(v.tensor_reduce(over_f[:, 1:N_OVER + 1], route[:, 24:24 + N_OVER, :], AX_X, ALU.add))
            link(v.tensor_scalar(over_f[:, 1:N_OVER + 1], over_f[:, 1:N_OVER + 1], float(NE - 1), None, ALU.min))
            link(v.tensor_scalar(over_f[:, N_LAST + 1:N_LAST + 2], incl[:, NE - 1:NE], 1.0, None, ALU.add))
            link(v.tensor_copy(over_i[:, :], over_f[:, :]))
            dve.wait_ge(wexp, TT)
            link(v.reciprocal(ssq[:, 0, :], ssq[:, 0, :]))
            link(v.tensor_tensor(topw[:, :, :], topw[:, :, :], ssq[:, 0, :].unsqueeze(2).to_broadcast([P, TT, TOPK]), ALU.mult))
            dve.wait_ge(tab_ps, 1)
            n_ = N_BLOCKS + 1
            link(v.tensor_scalar(tabf[:, 0, 0:n_], ps[:, 2, 0:n_], 0.0, float(NOWHERE), ALU.is_equal, ALU.mult))
            link(v.scalar_tensor_tensor(out=tabf[:, 1, 0:n_], in0=ps[:, 2, 0:n_], scalar=-1.0, in1=tabf[:, 0, 0:n_], op0=ALU.add, op1=ALU.add))
            link(v.tensor_copy(asg_i[:, :], tabf[:, 1, 0:n_]))
            v.tensor_scalar(tok_i[:, :], asg_i[:, :], 2, None, ALU.arith_shift_right).then_inc(tab_done, 1)

            def lo_w(b, i):
                dve.wait_ge(hi_done, b * MS + (W_MIX + i + 1))
                v.tensor_tensor(lo[i][:, :], raw[i][:, :], hi[i % HS][:, :].bitcast(F32), ALU.subtract).then_inc(split_done, 1)

            def lo_x(b, half):
                dve.wait_ge(xT_hi, b * 2 + (half + 1))
                h = slice(4 * half, 4 * half + 4)
                v.tensor_tensor(xT[1][:, h, :], ps[:, 6 + half, :].rearrange("p (k n) -> p k n", n=P),
                                xT[0][:, h, :].bitcast(F32), ALU.subtract).then_inc(xT_done, 1)

            def lo_a(b, half):
                dve.wait_ge(aT_hi, b * 2 + (half + 1))
                h = slice(4 * half, 4 * half + 4)
                v.tensor_tensor(aT[1][:, h, :], ps[:, 6 + half, :].rearrange("p (k n) -> p k n", n=P),
                                aT[0][:, h, :].bitcast(F32), ALU.subtract).then_inc(aT_done, 1)

            def glu(b, half, st):
                dve.wait_ge(chunk_used, b * MS + (W_MIX + 4 * half + 4))
                if half:
                    dve.wait_ge(glu_done, b * 2 + 1)
                v.tensor_scalar(gmin[:, :], ps[:, 2 * half, :], LIMIT, None, ALU.min)
                st(v.tensor_scalar(ucl[:, :], ps[:, 2 * half + 1, :], LIMIT, -LIMIT, ALU.min, ALU.max))
                st.wait()
                dve.wait_ge(sg_done, b * 2 + (half + 1))
                st(v.scalar_tensor_tensor(out=gmin[:, :], in0=sg[:, :], scalar=SIG_LIMIT, in1=gmin[:, :], op0=ALU.min, op1=ALU.mult))
                st.wait()
                v.scalar_tensor_tensor(out=act_h[:, half, :], in0=ucl[:, :], scalar=1.0, in1=gmin[:, :], op0=ALU.add, op1=ALU.mult).then_inc(glu_done, 1)

            st = Steps(dve, glu_step)

            def iteration(b, next_expert, more):
                st.n, st.at = 0, b * 4
                for i in range(3, MS):
                    if i == 11:
                        glu(b, 1, st)
                    lo_w(b, i)
                    if i == 6:
                        glu(b, 0, st)
                    if i == 8:
                        lo_a(b, 0)
                lo_x(b + 1, 0)
                more(lambda: lo_w(b + 1, 0))
                lo_a(b, 1)
                v.tensor_copy(sel[:, :], onehot[:, bass.DynSlice(next_expert(), 1)].to_broadcast([3 * NE, P])).then_inc(sel_done, 1)

                def two():
                    lo_w(b + 1, 1)
                    lo_w(b + 1, 2)
                more(two)
                lo_x(b + 1, 1)

            for i in range(3):
                lo_w(0, i)
            lo_x(0, 0)
            lo_x(0, 1)
            with dve.Fori(0, N_FIRST) as b:
                iteration(b, lambda: b + 1, lambda f: f())
            n_last = dve.value_load(over_i[0:1, N_LAST + 1:N_LAST + 2], min_val=1, max_val=N_LAST)
            with dve.Fori(0, N_LAST) as t:
                with dve.If(n_last > t):
                    def if_more(f):
                        with dve.If(n_last > t + 1):
                            f()
                    iteration(t + N_FIRST, lambda: dve.value_load(over_i[0:1, bass.DynSlice(t + 1, 1)], min_val=0, max_val=NE - 1), if_more)

            tl = Steps(dve, tail_step)
            for i in range(TT):
                c_ = comb[:, i % 2, :]
                dve.wait_ge(yk_in[i % 2], 32 * (i // 2 + 1))
                if i >= 2:
                    dve.wait_ge(out_done[i % 2], 16 * (i // 2))
                tl.link(v.tensor_scalar(c_, yk[:, i % 2, 0, :], topw[:, i, 0:1], None, ALU.mult))
                for k in range(1, TOPK):
                    ins = v.scalar_tensor_tensor(out=c_, in0=yk[:, i % 2, k, :], scalar=topw[:, i, k:k + 1], in1=c_, op0=ALU.mult, op1=ALU.add)
                    if k < TOPK - 1:
                        tl.link(ins)
                ins.then_inc(comb_done, 1)
                dve.wait_ge(t_ssq, 2 * i + 2)
                tl.link(v.reciprocal(ssq[:, 1, i:i + 1], ssq[:, 1, i:i + 1]))
                tl.link(v.scalar_tensor_tensor(out=c_, in0=c_, scalar=ssq[:, 1, i:i + 1], in1=gate_f[:, :], op0=ALU.mult, op1=ALU.mult))
                v.tensor_tensor(c_, c_, x2t[:, i % 2, :], ALU.add).then_inc(fin_done, 1)

        @block.tensor
        def _(pe):
            mm = nc.tensor.matmul
            PARTS = ((0, 0), (0, 1), (1, 0))

            def chunk(w):
                pe.wait_ge(split_done, w + 1)
                n = WEIGHTS[w]
                c = words(STREAM[n])
                return hi[hi_slot(w)][:, 0:c], lo[n % RS][:, 0:c]

            def feature_major(bank, parts, c0, acts, k0, kn, start, stop):
                for k in range(kn):
                    for q, (xa, wa) in enumerate(PARTS):
                        wk = parts[wa].rearrange("p (k n) -> p k n", k=kn)
                        last = mm(ps[:, bank, :], wk[:, k, c0:c0 + P], acts[xa][:, k0 + k, :],
                                  start=start and k == 0 and q == 0, stop=stop and k == kn - 1 and q == 2)
                return last

            pe.wait_ge(consts, 7)
            pe.wait_ge(rows_in, 16 * 8)
            nc.tensor.transpose(ps[:, 7, 0:R_END], rows[0:R_END, :], ident[0:R_END, 0:R_END]).then_inc(cols_ps, 1)
            pe.wait_ge(xn_done, TT)
            for k in range(KT):
                if k >= 4:
                    pe.wait_ge(htmp_done, k - 3)
                for i in range(TT):
                    last = nc.tensor.transpose(ps[:, k % 4, i * P:(i + 1) * P], xt[:, i, k * P:(k + 1) * P], ident[:, :])
                last.then_inc(tr_done, 1)
                if k == 3:
                    pe.wait_ge(ada_used, KT)
                    for c in range(2 * KT):
                        last = mm(ps[:, 6, c:c + 1], acc[0][:, c * P:(c + 1) * P], ones[:, 0:1], start=True, stop=True)
                    last.then_inc(mod_ps, 1)

            pe.wait_ge(hT_done, KT)
            for j in range(MT // 2):
                w = W_RNN + 2 * j
                parts = chunk(w)
                for m in (2 * j, 2 * j + 1):
                    if m >= 2:
                        pe.wait_ge(xrp_done, m - 1)
                    last = feature_major(m % 2, parts, (m % 2) * P, hT, 0, KT, True, True)
                    last.then_inc(chunk_used if m % 2 else x_ps, 1)
                parts = chunk(w + 1)
                for m in (2 * j, 2 * j + 1):
                    if m >= 4:
                        pe.wait_ge(g2_done, 2 * (m - 4) + 2)
                    last = feature_major(4 + m % 4, parts, (m % 2) * P, hT, 0, KT, True, True)
                    last.then_inc(chunk_used if m % 2 else g_ps, 1)
                if j == 0:
                    pe.wait_ge(gw_in, 16 * 2 * len(GATE_PIECES))
                pe.wait_ge(conv_done, 2 * j + 2)
                for m in READY[j]:
                    if m:
                        pe.wait_ge(gates_read, 2 * m)
                    pairs = [(q, k) for q, (k, mm_) in enumerate(PAIRS) if mm_ == m]
                    for which in range(2):
                        for n, (q, k) in enumerate(pairs):
                            last = mm(ps[:, 2 + which, :], gw[:, which, q, :], xc[:, k % 4, :], start=n == 0, stop=n == len(pairs) - 1)
                    last.then_inc(gates_ps, 1)

            def sums_over_partitions(acc_, bank0):
                for q in range(4):
                    mm(ps[:, bank0 + q, :], ones[:, :], acc_[:, q * 512:(q + 1) * 512], start=True, stop=True).then_inc(mod_ps, 1)

            for p in range(4):
                w = W_BR + 3 * p
                b0 = 4 * (p % 2)
                parts = chunk(w)
                if p == 0:
                    pe.wait_ge(gates_read, 2 * MT)
                    pe.wait_ge(xrp_done, MT)
                if p == 1:
                    pe.wait_ge(mod_done, 5)
                for t in (2 * p, 2 * p + 1):
                    if t >= 4:
                        pe.wait_ge(bm_done, t - 3)
                    feature_major(b0 + t % 2, parts, (t % 2) * P, hT, 0, KT, True, True).then_inc(chunk_used if t % 2 else bg_ps, 1)
                pe.wait_ge(rnn_lo, MT)
                for half in range(2):
                    parts = chunk(w + 1 + half)
                    for t in (2 * p, 2 * p + 1):
                        last = feature_major(b0 + 2 + t % 2, parts, (t % 2) * P, rnnT, half * (MT // 2), MT // 2, half == 0, half == 1)
                        if t % 2 or half:
                            last.then_inc(chunk_used if t % 2 else bp_ps, 1)
                if p == 0:
                    pe.wait_ge(ada_used, 2 * KT)
                    pe.wait_ge(g2_done, 2 * MT)
                    sums_over_partitions(acc[1], 4)
            pe.wait_ge(ada_used, 3 * KT)
            pe.wait_ge(bm_done, 6)
            sums_over_partitions(acc[2], 0)

            parts = chunk(W_KV)
            pe.wait_ge(mod_done, 9)
            feature_major(0, parts, 0, hT, 0, KT, True, True).then_inc(kv_ps, 1)
            for b in range(NC - 1):
                bank, c0 = 1 + b // 4, (b % 4) * P
                for k in range(KT):
                    for q, (xa, wa) in enumerate(PARTS):
                        wk = parts[wa].rearrange("p (k n) -> p k n", k=KT)
                        last = mm(ps[:, bank, c0:c0 + P], hT[xa][:, k, CHUNK * b:CHUNK * b + P], wk[:, k, P:2 * P],
                                  start=k == 0 and q == 0, stop=k == KT - 1 and q == 2)
            last.then_inc(chunk_used, 1)
            for g_ in range(NKV):
                for p in (2 * g_, 2 * g_ + 1):
                    parts = chunk(W_Q + p)
                    for t in (2 * p, 2 * p + 1):
                        if t == 0:
                            pe.wait_ge(bm_done, KT)
                        if t == 4:
                            pe.wait_ge(o_done, NC)
                        feature_major(4 + t % 4, parts, (t % 2) * P, hT, 0, KT, True, True).then_inc(chunk_used if t % 2 else q_ps, 1)
                pe.wait_ge(rope_done, 1 + 4 * (g_ + 1))
                if g_ == 0:
                    pe.wait_ge(kT_done, 4)
                    pe.wait_ge(v_done, 4)
                for c in range(NC + 1):
                    if c < NC:
                        u = NC * g_ + c
                        k0, n = (0, CHUNK) if c == 0 else (CHUNK * (c - 1), 2 * CHUNK)
                        if u >= 2:
                            pe.wait_ge(e_done, u - 1)
                        for jj in range(4):
                            last = mm(ps[:, u % 2, jj * P:jj * P + n], qbd[:, jj, c, :, :].rearrange("p h q -> p (h q)"),
                                      kT[:, g_, k0:k0 + n], start=True, stop=True)
                        last.then_inc(s_ps, 1)
                    if c:
                        u = NC * g_ + c - 1
                        n = CHUNK if c == 1 else 2 * CHUNK
                        pe.wait_ge(p_done, u + 1)
                        if u >= 2:
                            pe.wait_ge(pT_done, u - 1)
                        for jj in range(4):
                            last = nc.tensor.transpose(ps[0:n, 2 + u % 2, jj * P:(jj + 1) * P], prob[:, u % 2, jj, 0:n], ident[:, :])
                        last.then_inc(pT_ps, 1)
                        pe.wait_ge(pT_done, u + 1)
                        if u >= 2:
                            pe.wait_ge(o_done, u - 1)
                        b = max(c - 2, 0)
                        mm(ps[:, 4 + u % 2, :], vb[0:n, b, g_, :, :].rearrange("p t d -> p (t d)"),
                           probT[0:n, u % 2, :, :].rearrange("p j n -> p (j n)"), start=True, stop=True).then_inc(o_ps, 1)

            pe.wait_ge(o_done, 2 * NC)
            for p in range(4):
                w = W_BA + 2 * p
                b0 = 4 * (p % 2)
                for what in range(2):
                    parts = chunk(w + what)
                    for t in (2 * p, 2 * p + 1):
                        if t >= 4 and what == 0:
                            pe.wait_ge(mrg_sum, t - 3)
                        last = feature_major(b0 + 2 * what + t % 2, parts, (t % 2) * P, attnT if what else hT, 0, KT, True, True)
                        last.then_inc(chunk_used if t % 2 else (ap_ps if what else ag_ps), 1)

            for q in range(4):
                parts = chunk(W_OUT + q)
                pe.wait_ge(mrg_done, 2 * q + 2)
                if q == 0:
                    pe.wait_ge(mrg_sum, KT)
                for i in range(TT):
                    for h in range(2):
                        for kk in range(2):
                            for s_, (xa, wa) in enumerate(PARTS):
                                wk = parts[wa].rearrange("p (k n) -> p k n", k=2)
                                last = mm(ps[:, 2 * i + h, :], mrgT[xa][:, 2 * q + kk, i * P:(i + 1) * P], wk[:, kk, h * 512:(h + 1) * 512],
                                          start=q == 0 and kk == 0 and s_ == 0, stop=q == 3 and kk == 1 and s_ == 2,
                                          skip_group_check=True)
                last.then_inc(chunk_used, 1)

            for i in range(TT):
                pe.wait_ge(h2_done, i + 1)
                for k in range(KT):
                    last = nc.tensor.transpose(ps[:, 2 * i + k // 4, (k % 4) * P:(k % 4 + 1) * P], h2[:, i % 2, k * P:(k + 1) * P], ident[:, :])
                last.then_inc(h2_tr, 1)
                pe.wait_ge(hfT_done, i + 1)
                for k in range(KT):
                    last = mm(ps[:, 2 * i, 0:NE], hfT[:, k, :], wr[:, k, :], start=k == 0, stop=k == KT - 1)
                last.then_inc(lg_ps, 1)
            pe.wait_ge(mask_done, 1)
            mask = route[:, 4:8, :]
            for i in range(TT):
                for j in range(i + 1):
                    mm(ps[:, 0, i * NE:(i + 1) * NE], before[:, :] if j == i else ones[:, :], mask[:, j, :], start=j == 0, stop=j == i)
            for i in range(TT):
                last = mm(ps[:, 1, 0:NE], ones[:, :], mask[:, i, :], start=i == 0, stop=i == TT - 1)
            last.then_inc(rank_ps, 1)
            for q in range(TOPK * TT):
                pe.wait_ge(oh_done, q + 1)
                last = mm(ps[:, 2, 0:N_BLOCKS + 1], oh_slot[:, q, :], oh_blk[:, q, 0:N_BLOCKS + 1], start=q == 0, stop=q == TOPK * TT - 1)
            last.then_inc(tab_ps, 1)

            def turn_x(half):
                for k in range(4):
                    last = nc.tensor.transpose(ps[:, 6 + half, k * P:(k + 1) * P], xg[:, (4 * half + k) * P:(4 * half + k + 1) * P], ident[:, :])
                last.then_inc(xT_ps, 1)

            def turn_a(half):
                for k in range(4):
                    last = nc.tensor.transpose(ps[:, 6 + half, k * P:(k + 1) * P], act_h[:, half, k * P:(k + 1) * P], ident[:, :])
                last.then_inc(aT_ps, 1)

            def bias(bank, c0):
                mm(ps[:, bank, :], sel[:, :], bpart[:, c0:c0 + 512], start=True, stop=False)

            def expert_parts(i, kn):
                return [t[:, :].rearrange("p (k n) -> p k n", k=kn) for t in (hi[i % HS], lo[i])]

            def iteration(b):
                for i in range(8):
                    half, what, kk = i // 4, (i // 2) % 2, i % 2
                    bank = 2 * half + what
                    if i == 0:
                        pe.wait_ge(sel_done, b + 1)
                        pe.wait_ge(xT_done, b * 2 + 2)
                    pe.wait_ge(split_done, b * MS + (W_MIX + i + 1))
                    if kk == 0:
                        bias(bank, what * DE + half * 512)
                    wk = expert_parts(i, 4)
                    for k in range(4):
                        for q, (xa, wa) in enumerate(PARTS):
                            last = mm(ps[:, bank, :], xT[xa][:, 4 * kk + k, :], wk[wa][:, k, :], start=False, stop=kk == 1 and k == 3 and q == 2)
                    last.then_inc(chunk_used, 1)
                    if i == 5:
                        pe.wait_ge(glu_done, b * 2 + 1)
                        turn_a(0)
                for i in range(8, MS):
                    if i == 8:
                        pe.wait_ge(y_done, b + 1)
                        pe.wait_ge(aT_done, b * 2 + 1)
                        for h in range(2):
                            bias(4 + h, 2 * DE + h * 512)
                    if i == 10:
                        pe.wait_ge(aT_done, b * 2 + 2)
                    pe.wait_ge(split_done, b * MS + (W_MIX + i + 1))
                    wk = expert_parts(i, 2)
                    for k in range(2):
                        if i == 9 and k == 1:
                            pe.wait_ge(glu_done, b * 2 + 2)
                            turn_a(1)
                        for h in range(2):
                            for q, (xa, wa) in enumerate(PARTS):
                                last = mm(ps[:, 4 + h, :], aT[xa][:, 2 * (i - 8) + k, :], wk[wa][:, k, h * 512:(h + 1) * 512],
                                          start=False, stop=i == MS - 1 and k == 1 and q == 2)
                    last.then_inc(chunk_used, 1)
                    if i == 8:
                        pe.wait_ge(xg_in, b * 16 + 32)
                        turn_x(0)
                    if i == 10:
                        turn_x(1)

            pe.wait_ge(xg_in, 16)
            pe.wait_ge(xg_zero, 1)
            turn_x(0)
            turn_x(1)
            with pe.Fori(0, N_FIRST) as b:
                iteration(b)
            n_last = pe.value_load(over_i[0:1, N_LAST + 1:N_LAST + 2], min_val=1, max_val=N_LAST)
            with pe.Fori(0, N_LAST) as t:
                with pe.If(n_last > t):
                    iteration(t + N_FIRST)


_NAMES = ["x", "c", "positions", "w_ada", "b_ada", "g_pre_mix", "g_post_mix", "g_pre_ffn", "g_post_ffn", "w_in", "sinks",
          "conv_w", "conv_b", "w_rg_a", "b_rg_a", "w_rg_x", "b_rg_x", "rg_lambda", "w_branch_attn", "w_branch_rnn",
          "w_merge_gate", "b_merge_gate", "w_out", "w_router", "b_router", "w_e1", "b_e1", "w_e2", "b_e2"]


def kernel(**inputs):
    import numpy as _np
    import concourse.bacc as _bacc
    from concourse import mybir as _mybir
    from concourse.bass_utils import run_bass_kernel_spmd as _run

    nc = _bacc.Bacc("TRN2", target_bir_lowering=False, num_devices=1)
    arrays, args = {}, {}
    for name in _NAMES:
        arrays[name + "_dram"] = _np.ascontiguousarray(inputs[name])
    half = HD // 2
    freq = (10000.0 ** (-_np.arange(half) / half)).astype(_np.float32)
    arrays["inv_freq_dram"] = _np.ascontiguousarray(_np.concatenate([freq] * 4)[:, None])
    for name in _NAMES + ["inv_freq"]:
        arr = arrays[name + "_dram"]
        args[name] = nc.dram_tensor(name + "_dram", arr.shape, _mybir.dt.from_np(arr.dtype), kind="ExternalInput").ap()
    out = nc.dram_tensor("out_dram", (1, SEQ, D), F32, kind="ExternalOutput").ap()
    hybrid_block(nc, args, out)
    r = _run(nc, [arrays], core_ids=[0])
    return r.results[0]["out_dram"]
```

```python
from contextlib import ExitStack

import concourse.bass as bass
from concourse import mybir

ALU = mybir.AluOpType
ACT = mybir.ActivationFunctionType
F32 = mybir.dt.float32
F32R = mybir.dt.float32r
BF16 = mybir.dt.bfloat16
I32 = mybir.dt.int32
U32 = mybir.dt.uint32
AX_X = mybir.AxisListType.X

P = 128
KB = 1024
SEQ, D = 512, 1024
KT = D // P
TT = SEQ // P
CHUNK, HD, NQ, NKV = 64, 64, 16, 2
NC = SEQ // CHUNK
D_RNN, RB, NRB = 1280, 80, 16
MT = D_RNN // P
CONV = 4
NE, TOPK, DE = 32, 4, 1024
LIMIT, ALPHA = 7.0, 1.702
SIG_LIMIT = 0.9999933068838914
EPS = 1e-6
N_OVER = SEQ * TOPK // P
N_BLOCKS = NE + N_OVER
N_FIRST = NE - 1
N_LAST = N_BLOCKS - N_FIRST
NOWHERE = 1 << 20
QCOL, KCOL, VCOL, XCOL = 0, 1024, 1152, 1280
GCOL = XCOL + D_RNN
W = 256
CH = 2048
RS = 4
MS = 12
HS = 4

R_CONVW, R_BMG, R_GPM, R_C, R_CONVB, R_BA, R_BX, R_LAM, R_END = 0, 40, 56, 64, 72, 82, 92, 102, 112


def gate_pairs(m):
    lo, hi = (m * P // RB) * RB, -(-((m + 1) * P) // RB) * RB
    return list(range(lo // P, (hi - 1) // P + 1))


PAIRS = [(k, m) for m in range(MT) for k in gate_pairs(m)]
READY = [[m for m in range(MT) if max(gate_pairs(m)) // 2 == j] for j in range(MT // 2)]


HALF_PAIRS = len(PAIRS) // 2


def gate_pieces():
    out = []
    for q, (k, m) in enumerate(PAIRS[:HALF_PAIRS]):
        for b in range(NRB // 2):
            r0, r1 = max(b * RB, k * P), min((b + 1) * RB, (k + 1) * P)
            c0, c1 = max(b * RB, m * P), min((b + 1) * RB, (m + 1) * P)
            if r0 < r1 and c0 < c1:
                out.append((q, b, r0, r1, c0, c1))
    return out


GATE_PIECES = gate_pieces()


def stream_items():
    ada = [[("ada", part, k) for k in range(KT)] for part in range(3)]
    items = list(ada[0])
    for j in range(MT // 2):
        items.append(("in", XCOL + W * j))
        if ada[1]:
            items.append(ada[1].pop(0))
        items.append(("in", GCOL + W * j))
        if ada[1]:
            items.append(ada[1].pop(0))
    items.append(("mg", D))
    for p in range(4):
        if p < 3:
            items.append(("mg", D + W * (p + 1)))
        first, second = ada[2].pop(0), ada[2].pop(0)
        items += [("br", p, 0), first, ("br", p, 1), second] if p == 0 else [first, ("br", p, 0), ("br", p, 1), second]
    items.append(("in", KCOL))
    items += [("in", QCOL + W * p) for p in range(4)]
    items += [("mg", W * p) for p in range(4)]
    items += [("ba", p) for p in range(4)]
    items += [("out", p) for p in range(4)]
    return items


STREAM = stream_items()
WEIGHTS = [n for n, it in enumerate(STREAM) if it[0] != "ada"]
ADAS = [n for n, it in enumerate(STREAM) if it[0] == "ada"]
W_MIX = len(WEIGHTS)
W_RNN, W_BR, W_KV, W_Q, W_MG, W_BA, W_OUT = 0, 10, 22, 23, 27, 31, 35
assert W_OUT + 4 == W_MIX and (W_MIX + 1) % HS == 0


BR_GATE = [WEIGHTS.index(STREAM.index(("mg", D + W * p))) for p in range(4)]
BR_PROJ = [WEIGHTS.index(STREAM.index(("br", p, 0))) for p in range(4)]

NU = NKV * NC
FILL = {s: ("q", 4 + s) for s in range(4)}
FILL.update({s: ("mg", t) for t, s in enumerate((4, 5, 7, 8, 10, 11, 13, 14))})
SPLIT_AT = {2: W_MG, 4: W_MG + 1, 6: W_MG + 2, 7: W_MG + 3, 9: W_BA, 11: W_BA + 1, 13: W_BA + 2}


def hi_slot(w):
    return (w + 1) % HS


class Steps:

    def __init__(self, eng, sem):
        self.eng, self.sem, self.n, self.at = eng, sem, 0, None

    def __call__(self, ins):
        ins.then_inc(self.sem, 1)
        self.n += 1
        return ins

    def wait(self, back=0):
        n = self.n - back
        self.eng.wait_ge(self.sem, n if self.at is None else self.at + n)

    def link(self, ins):
        self(ins)
        self.wait()


def hybrid_block(nc, a, out):
    with ExitStack() as ctx:
        def sem(name):
            return ctx.enter_context(nc.semaphore(name))

        base = -(-nc.sbuf_base // 64) * 64
        end = nc.sbuf_usable_end
        top = [base]

        def put(name, shape, dt, off):
            return nc.alloc_sbuf_tensor_at(name, shape, dt, offset=off)

        def keep(name, shape, dt=F32):
            size = 2 if dt == BF16 else 4
            for s in shape[1:]:
                size *= s
            t = put(name, shape, dt, top[0])
            top[0] += -(-size // 32) * 32
            return t

        ident = keep("ident", [P, P])
        ones = keep("ones", [P, P])
        iota_f = keep("iota_f", [P, P])
        before = keep("before", [P, P])
        cols = keep("cols", [P, R_END])
        bcol = keep("bcol", [P, 36])
        scol = keep("scol", [P, KT])
        sp4 = keep("sp4", [P, 2, MT])
        modc = keep("modc", [P, 2, KT])
        small = keep("small", [P, 64])
        sink = keep("sink", [P, 8])
        eps = keep("eps", [P, 1])
        ticks = keep("ticks", [P, 4])
        freq = keep("freq", [P, 1])
        topw = keep("topw", [P, TT, TOPK])
        ssq = keep("ssq", [P, 4, TT])
        tok_i = keep("tok_i", [P, N_BLOCKS + 1], I32)
        asg_i = keep("asg_i", [P, N_BLOCKS + 1], I32)
        over_i = keep("over_i", [P, N_LAST + 2], I32)
        asgv = keep("asgv", [P, TOPK, TT])
        idx_now = keep("idx_now", [P, 2], I32)
        gate_m = keep("gate_m", [P, D])
        gate_f = keep("gate_f", [P, D])
        slots_at = top[0]
        hi_at = slots_at + RS * CH * 4
        zone = hi_at + HS * CH * 4
        assert zone + 131 * KB + 64 <= end

        def z(name, shape, dt, kb):
            return put(name, shape, dt, zone + int(kb * KB))

        slot_off = [slots_at + i * CH * 4 for i in range(RS)] + [zone + i * CH * 4 for i in range(MS - RS)]
        raw = [put(f"raw{i}", [P, CH], F32, slot_off[i]) for i in range(MS)]
        lo = [put(f"lo{i}", [P, CH], F32R, slot_off[i]) for i in range(MS)]
        hi = [put(f"hi{i}", [P, CH], F32R, hi_at + i * CH * 4) for i in range(HS)]

        hT = [z(f"hT{i}", [P, KT, SEQ], F32R, 16 * i) for i in range(2)]
        rnnT = [z(f"rnnT{i}", [P, MT, SEQ], F32R, 32 + 20 * i) for i in range(2)]
        mix = z("mix", [P, KT, SEQ], F32, 72)
        attn = z("attn", [P, KT, NC, 2, CHUNK], F32R, 88)
        xt = z("xt", [P, TT, D], F32, 88)
        rows = z("rows", [P, P], F32, 104)
        htmp = z("htmp", [P, 2, SEQ], F32, 106)
        xjunk = z("xjunk", [P, D], F32, 110)
        acc = [z("acc0", [P, 2 * D], F32, 114), z("acc1", [P, 2 * D], F32, 114), z("acc2", [P, 2 * D], F32, 92)]
        gw = z("gw", [P, 2, len(PAIRS), P], F32, 88)
        xc = z("xc", [P, 6, SEQ], F32, 68)
        th_a, th_i, dec, t_om = (z(n, [P, SEQ], F32, 80 + 2 * i) for i, n in enumerate(("th_a", "th_i", "dec", "t_om")))
        g2 = z("g2", [P, 2, SEQ], F32, 124)
        xrp = z("xrp", [P, SEQ + 4], F32, 128)
        gate_s = z("gate_s", [P, 2, SEQ], F32, 88)
        shift_f = z("shift_f", [P, D], F32, 123)
        scale_f = z("scale_f", [P, D], F32, 127)
        cos = z("cos", [P, SEQ], F32, 32)
        sin = z("sin", [P, SEQ], F32, 34)
        qbd = z("qbd", [P, KT, NC, 2, CHUNK], F32, 88)
        kT = z("kT", [P, NKV, SEQ], F32, 52)
        vb = z("vb", [P, NC - 1, NKV, 2, HD], F32, 56)
        rot = z("rot", [P, 2, SEQ], F32, 36)
        swp = z("swp", [P, 2, SEQ], F32, 40)
        prob = z("prob", [P, 2, 4, P], F32, 64)
        probT = z("probT", [P, 2, 4, P], F32, 68)
        kpos = z("kpos", [P, SEQ], I32, 70)
        gate_a = z("gate_a", [P, KT, SEQ], F32, 32)
        mtmp = z("mtmp", [P, 2, SEQ], F32, 68)
        mrgT = [z(f"mrgT{i}", [P, KT, SEQ], F32R, 32 + 16 * i) for i in range(2)]
        x2 = z("x2", [P, TT, D], F32, 64)
        h2 = [z(f"h2_{i}", [P, D], F32, kb) for i, kb in enumerate((80, 84, 94))]
        hfT = z("hfT", [P, KT, P], F32, 88)
        mixed = z("mixed", [P, D], F32, 118)
        junk = z("junk", [P, D], BF16, 92)
        btab = z("btab", [NE, 3 * DE], F32, 96)
        bpart = z("bpart", [3 * NE, 3 * DE], BF16, 108)
        wr = z("wr", [P, KT, NE], F32, 114)
        brt = z("brt", [P, NE], F32, 115)
        bt16 = z("bt16", [NE, 3 * DE], BF16, 88)
        top8 = z("top8", [P, TT, 8], F32, 104)
        idx8 = z("idx8", [P, TT, 8], U32, 104.25)
        idxf = z("idxf", [P, TT, 8], F32, 104.5)
        pick = z("pick", [P, 2, TOPK * TT], F32, 104.75)
        over_f = z("over_f", [P, N_LAST + 2], F32, 105)
        ohe = z("ohe", [P, 2, TOPK * TT, NE], F32, 118)
        oh_slot = z("oh_slot", [P, TOPK * TT, P], F32, 64)
        oh_blk = z("oh_blk", [P, TOPK * TT, 64], F32, 72)
        tabf = z("tabf", [P, 2, 64], F32, 76)
        route = z("route", [P, 40, NE], F32, 98)
        xg = z("xg", [P, D], F32, 64)
        xT = [z(f"xT{i}", [P, KT, P], F32R, 68 + 4 * i) for i in range(2)]
        sg, gmin, ucl = (z(n, [P, 512], F32, 76 + 2 * i) for i, n in enumerate(("sg", "gmin", "ucl")))
        act_h = z("act_h", [P, 2, 512], F32, 82)
        aT = [z(f"aT{i}", [P, KT, P], F32R, 86 + 4 * i) for i in range(2)]
        ysb = z("ysb", [P, D], F32, 94)
        sel = z("sel", [3 * NE, P], BF16, 116)
        onehot = z("onehot", [3 * NE, NE], BF16, 117)
        yk = z("yk", [P, TT, TOPK, D], F32, 0)
        comb = z("comb", [P, TT, D], F32, 64)
        tjunk = z("tjunk", [P, D], F32, 80)
        x2t = [z(f"x2t{i}", [P, 2, D], F32, (98, 118)[i]) for i in range(2)]

        ps = ctx.enter_context(nc.psum_tensor("ps", [P, 8, 512], F32))

        h2_d = nc.dram_tensor("h2_d", (SEQ, D), F32).ap()
        x2_d = nc.dram_tensor("x2_d", (SEQ, D), F32).ap()
        yk_d = nc.dram_tensor("yk_d", (SEQ * TOPK, D), F32).ap()

        chunk_in = [sem(f"chunk_in{i}") for i in range(MS)]
        hi_done = sem("hi_done")
        split_done = sem("split_done")
        chunk_used = sem("chunk_used")
        ada_used = sem("ada_used")
        small_in = sem("small_in")
        rows_in = sem("rows_in")
        x_in = sem("x_in")
        acc_in = [sem(f"acc_in{i}") for i in range(3)]
        acc_zero = sem("acc_zero")
        consts = sem("consts")
        gw_zero = sem("gw_zero")
        gw_in = [sem(f"gw_in{i}") for i in range(2)]
        dve_step = sem("dve_step")
        cols_ps = sem("cols_ps")
        cols_done = sem("cols_done")
        cexp = sem("cexp")
        scol_done = sem("scol_done")
        ssq_done = sem("ssq_done")
        rms_done = sem("rms_done")
        xn_done = sem("xn_done")
        mod_ps = sem("mod_ps")
        mod_done = sem("mod_done")
        tr_done = sem("tr_done")
        htmp_done = sem("htmp_done")
        hT_hi = sem("hT_hi")
        hT_done = sem("hT_done")
        sp_exp = sem("sp_exp")
        sp_done = sem("sp_done")
        x_ps = sem("x_ps")
        xrp_done = sem("xrp_done")
        conv_done = sem("conv_done")
        g_ps = sem("g_ps")
        gates_ps = sem("gates_ps")
        gates_read = sem("gates_read")
        a_done = sem("a_done")
        om_done = sem("om_done")
        sqrt_done = sem("sqrt_done")
        g2_done = sem("g2_done")
        inner_done = sem("inner_done")
        gelu_th = sem("gelu_th")
        gelu_done = sem("gelu_done")
        rnn_done = sem("rnn_done")
        rnn_hi = sem("rnn_hi")
        rnn_lo = sem("rnn_lo")
        bg_ps = sem("bg_ps")
        bg_done = sem("bg_done")
        bp_ps = sem("bp_ps")
        ag_ps = sem("ag_ps")
        ap_ps = sem("ap_ps")
        bm_done = sem("bm_done")
        pos_in = sem("pos_in")
        ang_done = sem("ang_done")
        trig_done = sem("trig_done")
        kv_ps = sem("kv_ps")
        q_ps = sem("q_ps")
        swp_done = sem("swp_done")
        rope_done = sem("rope_done")
        kT_done = sem("kT_done")
        v_done = sem("v_done")
        qbd_zero = sem("qbd_zero")
        s_ps = sem("s_ps")
        m_done = sem("m_done")
        e_done = sem("e_done")
        p_done = sem("p_done")
        pT_ps = sem("pT_ps")
        pT_done = sem("pT_done")
        o_ps = sem("o_ps")
        o_hi = sem("o_hi")
        o_done = sem("o_done")
        mrg_sum = sem("mrg_sum")
        mrg_hi = sem("mrg_hi")
        mrg_done = sem("mrg_done")
        e_ssq = sem("e_ssq")
        e_rms = sem("e_rms")
        n_rms = sem("n_rms")
        xe_in = sem("xe_in")
        x2_done = sem("x2_done")
        h2_done = sem("h2_done")
        h2_out = [sem(f"h2_out{i}") for i in range(TT)]
        x2_out = sem("x2_out")
        h2_tr = sem("h2_tr")
        hfT_done = sem("hfT_done")
        lg_ps = sem("lg_ps")
        bt_in = sem("bt_in")
        bpart_done = sem("bpart_done")
        mask_done = sem("mask_done")
        rank_ps = sem("rank_ps")
        wexp = sem("wexp")
        wsub = sem("wsub")
        oh_done = sem("oh_done")
        tab_ps = sem("tab_ps")
        tab_done = sem("tab_done")
        over_done = sem("over_done")
        xg_in = sem("xg_in")
        xg_zero = sem("xg_zero")
        xT_ps = sem("xT_ps")
        xT_hi = sem("xT_hi")
        xT_done = sem("xT_done")
        sel_done = sem("sel_done")
        glu_step = sem("glu_step")
        sg_done = sem("sg_done")
        glu_done = sem("glu_done")
        aT_ps = sem("aT_ps")
        aT_hi = sem("aT_hi")
        aT_done = sem("aT_done")
        y_done = sem("y_done")
        y_out = sem("y_out")
        ysb_free = sem("ysb_free")
        gpost_in = sem("gpost_in")
        idx_done = sem("idx_done")
        yk_in = [sem(f"yk_in{i}") for i in range(TT)]
        x2t_in = sem("x2t_in")
        comb_done = sem("comb_done")
        t_ssq = sem("t_ssq")
        fin_done = sem("fin_done")
        out_done = sem("out_done")
        tail_step = sem("tail_step")

        w_in, w_mg, w_ba, w_br, w_out = (a[n][0] for n in ("w_in", "w_merge_gate", "w_branch_attn", "w_branch_rnn", "w_out"))
        w_e1, w_e2 = a["w_e1"], a["w_e2"]
        x_tok = a["x"][0].rearrange("(i p) d -> p i d", p=P)

        def chunk_src(it):
            if it[0] == "ada":
                return a["w_ada"][0][it[2] * P:(it[2] + 1) * P, it[1] * CH:(it[1] + 1) * CH], None
            if it[0] == "in":
                return w_in[:, it[1]:it[1] + W].rearrange("(k p) n -> p k n", p=P), KT
            if it[0] == "mg":
                return w_mg[:, it[1]:it[1] + W].rearrange("(k p) n -> p k n", p=P), KT
            if it[0] == "ba":
                return w_ba[:, it[1] * W:(it[1] + 1) * W].rearrange("(k p) n -> p k n", p=P), KT
            if it[0] == "br":
                h = MT // 2
                return w_br[it[2] * h * P:(it[2] + 1) * h * P, it[1] * W:(it[1] + 1) * W].rearrange("(k p) n -> p k n", p=P), h
            return w_out[it[1] * 2 * P:(it[1] + 1) * 2 * P, :].rearrange("(k p) n -> p k n", p=P), 2

        def tile_ready(eng, first, t, w):
            if t % 2 == 0:
                eng.wait_ge(first, t // 2 + 1)
            else:
                eng.wait_ge(chunk_used, w + 1)

        def gate_bank(t):
            return (0, 6)[t // 2 % 2] + t % 2

        def proj_bank(t):
            return (2, 4)[t // 2 % 2] + t % 2

        def q_bank(t):
            return 4 + t if t < 4 else 6 + t % 2

        def words(it):
            return (MT // 2) * W if it[0] == "br" else CH

        last_use = {}
        for n in range(len(STREAM)):
            last_use[n % RS] = n
        mix_uses = [len([n for n in range(len(STREAM)) if n % RS == i]) if i < RS else 0 for i in range(MS)]

        def slot_free(eng, n):
            if STREAM[n][0] == "ada":
                eng.wait_ge(ada_used, ADAS.index(n) + 1)
            else:
                eng.wait_ge(chunk_used, WEIGHTS.index(n) + 1)

        def expert_src(e, i):
            if i < 8:
                half, what, kk = i // 4, (i // 2) % 2, i % 2
                c0 = what * DE + half * 512
                return w_e1[0, e, kk * 512:(kk + 1) * 512, c0:c0 + 512].rearrange("o (k p) n -> p (o k) n", p=P)
            r0 = (i - 8) * 256
            return w_e2[0, e, r0:r0 + 256, :].rearrange("o (k p) n -> p (o k) n", p=P)

        def expert_dst(i):
            return raw[i][:, :].rearrange("p (k n) -> p k n", k=4 if i < 8 else 2)

        def load_gate_weights(eng, which):
            eng.wait_ge(gw_zero, which + 1)
            for q, b, r0, r1, c0, c1 in GATE_PIECES:
                k, m = PAIRS[q]
                eng.dma_start(gw[r0 - k * P:r1 - k * P, which, q::HALF_PAIRS, c0 - m * P:c1 - m * P],
                              a[("w_rg_a", "w_rg_x")[which]][0, b::NRB // 2, r0 - b * RB:r1 - b * RB, c0 - b * RB:c1 - b * RB]
                              .rearrange("b p n -> p b n")).then_inc(gw_in[which], 16)

        block = ctx.enter_context(nc.Block())

        @block.sync
        def _(sp):
            sp.dma_start(rows[R_CONVW:R_CONVW + CONV * MT, :], a["conv_w"][0].rearrange("j (r c) -> (j r) c", c=P)).then_inc(rows_in, 16)
            for r0, name in ((R_BA, "b_rg_a"), (R_BX, "b_rg_x")):
                sp.dma_start(rows[r0:r0 + MT, :], a[name][0].rearrange("b j -> (b j)").rearrange("(r c) -> r c", c=P)).then_inc(rows_in, 16)
            for n, it in enumerate(STREAM):
                if n >= RS:
                    slot_free(sp, n - RS)
                src, k = chunk_src(it)
                dst = raw[n % RS][:, 0:words(it)]
                if k is not None:
                    dst = dst.rearrange("p (k n) -> p k n", k=k)
                sp.dma_start(dst, src).then_inc(chunk_in[n % RS], 16)
                if n == KT + RS - 1:
                    load_gate_weights(sp, 0)

            sp.wait_ge(chunk_used, W_BA)
            for i in list(range(RS, 8)) + list(range(RS)) + list(range(8, MS)):
                if i < RS:
                    slot_free(sp, last_use[i])
                elif i == 8:
                    sp.wait_ge(chunk_used, W_MIX)
                sp.dma_start(expert_dst(i), expert_src(bass.DynSlice(0, 1), i)).then_inc(chunk_in[i], 16)
            sp.wait_ge(over_done, 1)
            sp.wait_ge(x2_out, 16)
            sp.wait_ge(xg_in, 16)
            for i in range(2):
                sp.dma_start(x2t[i][:, :, :], x2_d[i * 2 * P:(i + 1) * 2 * P, :].rearrange("(i p) d -> p i d", p=P)).then_inc(x2t_in, 16)

            def load_expert(e, b):
                for i in range(MS):
                    sp.wait_ge(chunk_used, b * MS + (W_MIX - MS + i + 1))
                    sp.dma_start(expert_dst(i), expert_src(bass.DynSlice(e, 1), i)).then_inc(chunk_in[i], 16)

            with sp.Fori(1, N_FIRST) as b:
                load_expert(b, b)
            sp.wait_ge(over_done, 1)
            n_last = sp.value_load(over_i[0:1, N_LAST + 1:N_LAST + 2], min_val=1, max_val=N_LAST)
            with sp.Fori(0, N_LAST) as t:
                with sp.If(n_last > t):
                    e = sp.value_load(over_i[0:1, bass.DynSlice(t, 1)], min_val=0, max_val=NE - 1)
                    load_expert(e, t + N_FIRST)
            yk_rows = yk_d.rearrange("(i p k) d -> i p k d", p=P, k=TOPK)
            out_tok = out[0].rearrange("(i p) d -> i p d", p=P)
            sp.wait_ge(y_out, n_last * 16 + 16 * N_FIRST)
            for i in range(TT):
                sp.dma_start(yk[:, i, :, :], yk_rows[i]).then_inc(yk_in[i], 16)
            for i in range(TT):
                sp.wait_ge(fin_done, i + 1)
                sp.dma_start(out_tok[i], comb[:, i, :]).then_inc(out_done, 16)
            sp.wait_ge(out_done, 16 * TT)

        @block.gpsimd
        def _(pool):
            g = nc.gpsimd
            g.memset(ident[:, :], 0.0).then_inc(consts, 1)
            g.memset(ones[:, :], 1.0).then_inc(consts, 1)
            g.memset(eps[:, :], EPS).then_inc(consts, 1)
            g.iota(iota_f[:, :], pattern=[[1, P]], base=0, channel_multiplier=0,
                   allow_small_or_imprecise_dtypes=True).then_inc(consts, 1)
            g.memset(acc[0][:, :], 0.0).then_inc(acc_zero, 1)
            pool.wait_ge(acc_zero, 1)
            pool.dma_start(acc[0][0:1, :], a["b_ada"][0:1, 0:CH]).then_inc(acc_in[0], 16)
            pool.wait_ge(consts, 4)
            g.affine_select(out=ident[:, :], in_=ident[:, :], compare_op=ALU.not_equal, fill=1.0, base=0,
                            pattern=[[-1, P]], channel_multiplier=1).then_inc(consts, 1)
            g.iota(asgv[:, :, :], pattern=[[1, TOPK], [P * TOPK, TT]], base=1, channel_multiplier=TOPK,
                   allow_small_or_imprecise_dtypes=True).then_inc(consts, 1)
            g.affine_select(out=before[:, :], in_=ones[:, :], compare_op=ALU.is_gt, fill=0.0, base=0,
                            pattern=[[1, P]], channel_multiplier=-1).then_inc(consts, 1)
            pool.wait_ge(mod_done, 1)
            g.memset(acc[1][:, :], 0.0).then_inc(acc_zero, 1)
            pool.wait_ge(acc_zero, 2)
            pool.dma_start(acc[1][0:1, :], a["b_ada"][0:1, CH:2 * CH]).then_inc(acc_in[1], 16)
            pool.wait_ge(tr_done, KT)
            g.memset(gw[:, 0, :, :], 0.0).then_inc(gw_zero, 1)
            pool.wait_ge(hT_done, KT)
            g.memset(gw[:, 1, :, :], 0.0).then_inc(gw_zero, 1)
            g.memset(xrp[:, 0:CONV - 1], 0.0).then_inc(gw_zero, 1)
            load_gate_weights(pool, 1)
            pool.wait_ge(gates_ps, MT)
            g.memset(acc[2][:, :], 0.0).then_inc(acc_zero, 1)
            pool.wait_ge(acc_zero, 3)
            pool.dma_start(acc[2][0:1, :], a["b_ada"][0:1, 2 * CH:3 * CH]).then_inc(acc_in[2], 16)
            pool.wait_ge(bm_done, KT)
            pool.wait_ge(mod_ps, 9)
            g.memset(qbd[0:64, :, :, 1, :], 0.0).then_inc(qbd_zero, 1)
            g.memset(qbd[64:128, :, :, 0, :], 0.0).then_inc(qbd_zero, 1)

            pool.wait_ge(tab_done, 1)
            for i in range(TT):
                pool.wait_ge(h2_out[i], 16)
            g.memset(xg[:, :], 0.0).then_inc(xg_zero, 1)
            pool.wait_ge(xg_zero, 1)

            def gather(at):
                g.tensor_copy(idx_now[:, 0:1], tok_i[:, at:at + 1]).then_inc(idx_done, 1)

            def gather_dma():
                pool.indirect_dma_start(out=xg[:, :], out_offset=None, in_=h2_d[:, :],
                                        in_offset=bass.IndirectOffsetOnAxis(ap=idx_now[:, 0:1].bitcast(U32), axis=0),
                                        bounds_check=SEQ - 1, oob_is_err=False).then_inc(xg_in, 16)

            def scatter_dma():
                pool.indirect_dma_start(out=yk_d[:, :], out_offset=bass.IndirectOffsetOnAxis(
                    ap=idx_now[:, 1:2].bitcast(U32), axis=0), in_=ysb[:, :], in_offset=None,
                                        bounds_check=SEQ * TOPK - 1, oob_is_err=False).then_inc(y_out, 16)

            gather(0)
            pool.wait_ge(idx_done, 1)
            gather_dma()

            def tick(n):
                return g.tensor_tensor(ticks[:, n:n + 1], eps[:, :], eps[:, :], ALU.add)

            def iteration(b, first=False):
                pool.wait_ge(xT_ps, b * 2 + 2)
                pool.wait_ge(xg_in, b * 16 + 16)
                g.tensor_copy(idx_now[:, 0:1], tok_i[:, bass.DynSlice(b + 1, 1)]).then_inc(idx_done, 1)
                pool.wait_ge(idx_done, b * 2 + 2)
                tick(0)
                gather_dma()
                if not first:
                    pool.wait_ge(y_out, b * 16)
                tick(2).then_inc(ysb_free, 1)
                g.tensor_copy(idx_now[:, 1:2], asg_i[:, bass.DynSlice(b, 1)]).then_inc(idx_done, 1)
                pool.wait_ge(idx_done, b * 2 + 3)
                pool.wait_ge(y_done, b + 2)
                tick(1)
                scatter_dma()

            iteration(0, first=True)
            with pool.Fori(1, N_FIRST) as b:
                iteration(b)
            pool.wait_ge(over_done, 1)
            n_last = pool.value_load(over_i[0:1, N_LAST + 1:N_LAST + 2], min_val=1, max_val=N_LAST)
            with pool.Fori(0, N_LAST) as t:
                with pool.If(n_last > t):
                    iteration(t + N_FIRST)

        @block.scalar
        def _(act):
            s = nc.scalar

            act.dma_start(rows[R_C:R_C + KT, :], a["c"].rearrange("o (r c) -> (o r) c", c=P)).then_inc(rows_in, 16)
            for r0, name, sz in ((R_BMG, "b_merge_gate", 16), (R_GPM, "g_pre_mix", 8),
                                 (R_CONVB, "conv_b", MT), (R_LAM, "rg_lambda", MT)):
                act.dma_start(rows[r0:r0 + sz, :], a[name].rearrange("o (r c) -> (o r) c", c=P)).then_inc(rows_in, 16)
            act.dma_start(xt[:, :, :], x_tok).then_inc(x_in, 16)
            act.wait_ge(cols_done, 1)
            s.activation(small[:, 0:8], cols[:, R_C:R_C + 8], ACT.Exp, scale=-1.0).then_inc(cexp, 1)
            act.wait_ge(x_in, 16)
            for i in range(TT):
                if i:
                    act.wait_ge(ssq_done, i)
                s.activation(xjunk[:, :], xt[:, i, :], ACT.Square, accum_out=ssq[:, 0, i:i + 1]).then_inc(ssq_done, 1)
            act.wait_ge(ssq_done, TT)
            act.wait_ge(consts, 4)
            s.activation(ssq[:, 1, :], ssq[:, 0, :], ACT.Sqrt, bias=eps[:, 0:1], scale=1.0 / D).then_inc(rms_done, 1)
            def round_hi(w):
                if w >= W_MIX:
                    return
                n = WEIGHTS[w]
                c = words(STREAM[n])
                act.wait_ge(chunk_in[n % RS], 16 * (n // RS + 1))
                if w >= HS:
                    act.wait_ge(chunk_used, w - HS + 1)
                s.activation(hi[hi_slot(w)][:, 0:c], raw[n % RS][:, 0:c], ACT.Copy).then_inc(hi_done, 1)

            round_hi(0)
            for k in range(KT):
                act.wait_ge(htmp_done, k + 1)
                s.activation(hT[0][:, k, :], htmp[:, k % 2, :], ACT.Copy).then_inc(hT_hi, 1)
            round_hi(1)
            act.wait_ge(sp_exp, 1)
            s.activation(small[:, 20:30], small[:, 10:20], ACT.Exp, scale=-1.0).then_inc(cexp, 1)
            act.dma_start(gate_m[:, :], a["g_post_mix"].to_broadcast([P, D])).then_inc(gpost_in, 16)
            act.dma_start(gate_f[:, :], a["g_post_ffn"].to_broadcast([P, D])).then_inc(gpost_in, 16)
            sk = a["sinks"].rearrange("o (t h) -> h o t", h=2)
            for h in range(2):
                act.dma_start(sink[64 * h:64 * h + 64, :], sk[h].to_broadcast([64, 8]), allow_slow_non_contiguous=True).then_inc(small_in, 16)

            act.dma_start(freq[:, :], a["inv_freq"][:, :]).then_inc(small_in, 16)

            def conv_rows(j):
                for m in (2 * j, 2 * j + 1):
                    tile_ready(act, x_ps, m, 2 * j)
                    if m:
                        act.wait_ge(conv_done, m)
                    s.activation(xrp[:, CONV - 1:CONV - 1 + SEQ], ps[:, m % 2, :], ACT.Copy).then_inc(xrp_done, 1)

            def gelu_square(m):
                tile_ready(act, g_ps, m, 2 * (m // 2) + 1)
                if m >= 2:
                    act.wait_ge(rnn_lo, m - 1)
                s.activation(g2[:, m % 2, :], ps[:, 4 + m % 4, :], ACT.Square).then_inc(g2_done, 1)

            conv_rows(0)
            round_hi(2)
            round_hi(3)
            gelu_square(0)
            act.wait_ge(sp_done, 1)
            for j in range(MT // 2):
                if 2 * j + 2 < MT:
                    conv_rows(j + 1)
                for m in READY[j]:
                    act.wait_ge(gates_ps, m + 1)
                    if m:
                        act.wait_ge(rnn_done, m)
                    s.activation(th_a[:, :], ps[:, 2, :], ACT.Tanh, bias=bcol[:, 16 + m:17 + m], scale=0.5).then_inc(gates_read, 1)
                    s.activation(th_i[:, :], ps[:, 3, :], ACT.Tanh, bias=bcol[:, 26 + m:27 + m], scale=0.5).then_inc(gates_read, 1)
                    act.wait_ge(gates_read, 2 * m + 1)
                    s.activation(dec[:, :], th_a[:, :], ACT.Exp, bias=sp4[:, 1, m:m + 1], scale=sp4[:, 1, m:m + 1]).then_inc(a_done, 1)
                    s.activation(t_om[:, :], th_a[:, :], ACT.Tanh, bias=sp4[:, 0, m:m + 1], scale=sp4[:, 0, m:m + 1]).then_inc(a_done, 1)
                    act.wait_ge(a_done, 3 * m + 2)
                    s.activation(th_a[:, :], dec[:, :], ACT.Square).then_inc(a_done, 1)
                    act.wait_ge(inner_done, m + 1)
                    s.activation(g2[:, m % 2, :], g2[:, m % 2, :], ACT.Tanh, scale=0.7978845608028654).then_inc(gelu_th, 1)
                    act.wait_ge(om_done, m + 1)
                    s.activation(t_om[:, :], t_om[:, :], ACT.Sqrt).then_inc(sqrt_done, 1)
                    if m + 1 < MT:
                        gelu_square(m + 1)
                    if m == READY[j][0]:
                        round_hi(2 * j + 4)
                    act.wait_ge(rnn_done, m + 1)
                    s.activation(rnnT[0][:, m, :], g2[:, m % 2, :], ACT.Copy).then_inc(rnn_hi, 1)
                    if m == READY[j][-1] and j < MT // 2 - 1 or m == MT - 2:
                        round_hi(2 * j + 5)

            act.wait_ge(rnn_lo, MT)
            act.dma_start(scale_f[:, :], a["g_pre_ffn"].to_broadcast([P, D])).then_inc(gpost_in, 16)
            for p in range(4):
                for t in (2 * p, 2 * p + 1):
                    tile_ready(act, bg_ps, t, BR_GATE[p])
                    if t >= 2:
                        act.wait_ge(bm_done, t - 1)
                    s.activation(gate_s[:, t % 2, :], ps[:, gate_bank(t), :], ACT.Tanh,
                                 bias=bcol[:, 8 + t:9 + t], scale=0.5).then_inc(bg_done, 1)
                for w in range(BR_PROJ[0] + 3 * p + 2, min(BR_PROJ[0] + 3 * p + 5, W_Q + 1)):
                    round_hi(w)

            act.wait_ge(bm_done, KT)
            act.dma_start(kpos[:, :], a["positions"].to_broadcast([P, SEQ])).then_inc(pos_in, 16)
            act.wait_ge(ang_done, 1)
            s.activation(cos[:, :], cos[:, :], ACT.Sin).then_inc(trig_done, 1)
            act.wait_ge(ang_done, 2)
            s.activation(sin[:, :], sin[:, :], ACT.Sin).then_inc(trig_done, 1)

            def swap_halves(bank, r):
                for q in range(4):
                    last = s.activation(swp[32 * q:32 * q + 32, r, :], ps[32 * (q ^ 1):32 * (q ^ 1) + 32, bank, :], ACT.Copy)
                last.then_inc(swp_done, 1)

            act.wait_ge(kv_ps, 1)
            swap_halves(0, 0)
            act.wait_ge(rope_done, 1)
            for g_ in range(NKV):
                for h in range(2):
                    s.activation(kT[64 * h:64 * h + 64, g_, :], rot[64 * g_:64 * g_ + 64, 0, :], ACT.Copy).then_inc(kT_done, 1)
            round_hi(W_Q + 1)
            act.wait_ge(chunk_used, W_KV + 1)
            for twice in range(2):
                for bank, b0, nb in ((1, 0, 4), (2, 4, 3)):
                    s.activation(vb[:, b0:b0 + nb, :, twice, :],
                                 ps[:, bank, 0:nb * P].rearrange("p (b g d) -> p b g d", g=NKV, d=HD), ACT.Copy).then_inc(v_done, 1)
            round_hi(W_Q + 2)

            def swap_q(t):
                tile_ready(act, q_ps, t, W_Q + t // 2)
                if t:
                    act.wait_ge(rope_done, t)
                swap_halves(q_bank(t), (t + 1) % 2)

            for t in range(4):
                swap_q(t)
                if t == 1:
                    round_hi(W_Q + 3)
            for step_ in range(NU + 3):
                u = step_
                if u < NU:
                    n = CHUNK if u % NC == 0 else 2 * CHUNK
                    o = 8 * (u % 2)
                    act.wait_ge(m_done, u + 1)
                    if u >= 2:
                        act.wait_ge(pT_ps, u - 1)
                    for jj in range(4):
                        s.activation(prob[:, u % 2, jj, 0:n], ps[:, u % 2, jj * P:jj * P + n], ACT.Exp,
                                     bias=small[:, o + jj:o + jj + 1], scale=HD ** -0.5,
                                     accum_out=small[:, 16 + o + jj:17 + o + jj])
                    s.activation(small[:, 32 + o:36 + o], small[:, 4 + o:8 + o], ACT.Exp).then_inc(e_done, 1)
                u = step_ - 2
                if 0 <= u < NU:
                    n = CHUNK if u % NC == 0 else 2 * CHUNK
                    act.wait_ge(pT_ps, u + 1)
                    if u >= 2:
                        act.wait_ge(o_ps, u - 1)
                    s.activation(probT[0:n, u % 2, :, :], ps[0:n, 2 + u % 2, :].rearrange("p (j n) -> p j n", n=P), ACT.Copy).then_inc(pT_done, 1)
                u = step_ - 3
                if u >= 0:
                    g_, c = u // NC, u % NC
                    act.wait_ge(o_ps, u + 1)
                    for h in range(2):
                        s.activation(attn[64 * h:64 * h + 64, 4 * g_:4 * g_ + 4, c, 0, :],
                                     ps[64 * h:64 * h + 64, 4 + u % 2, :].rearrange("p (j h q) -> p j h q", h=2, q=CHUNK)[:, :, h, :],
                                     ACT.Copy).then_inc(o_hi, 1)
                if step_ in SPLIT_AT:
                    round_hi(SPLIT_AT[step_])
                what, t = FILL.get(step_ - 1, (None, 0))
                if what == "q":
                    swap_q(t)
                elif what == "mg":
                    tile_ready(act, ag_ps, t, W_MG + t // 2)
                    s.activation(gate_a[:, t, :], ps[:, 6 + t % 2, :], ACT.Tanh, bias=bcol[:, t:t + 1], scale=0.5).then_inc(bg_done, 1)
            round_hi(W_BA + 3)

            for t in range(KT):
                act.wait_ge(mrg_sum, t + 1)
                s.activation(mrgT[0][:, t, :], mtmp[:, t % 2, :], ACT.Copy, scale=0.5).then_inc(mrg_hi, 1)
                if t % 2 and t >= 3:
                    round_hi(W_OUT + t // 2 - 1)
            round_hi(W_OUT + 3)
            act.wait_ge(mrg_done, KT)
            act.dma_start(x2[:, :, :], x_tok).then_inc(xe_in, 16)
            act.dma_start(btab[:, 0:2 * DE], a["b_e1"][0]).then_inc(bt_in, 16)
            act.dma_start(btab[:, 2 * DE:3 * DE], a["b_e2"][0]).then_inc(bt_in, 16)
            act.dma_start(wr[:, :, :], a["w_router"][0].rearrange("(k p) n -> p k n", p=P)).then_inc(bt_in, 16)
            act.dma_start(brt[:, :], a["b_router"].to_broadcast([P, NE])).then_inc(bt_in, 16)
            act.wait_ge(bpart_done, 1)
            act.wait_ge(chunk_used, W_MIX)
            squares = [0]

            def square_sum(src, dst):
                if squares[0]:
                    act.wait_ge(e_ssq, squares[0])
                s.activation(junk[:, :] if len(src.shape) == 2 else junk[:, :].rearrange("p (b n) -> p b n", b=2),
                             src, ACT.Square, accum_out=dst).then_inc(e_ssq, 1)
                squares[0] += 1
                act.wait_ge(e_ssq, squares[0])

            def post_norm(i):
                square_sum(ps[:, 2 * i:2 * i + 2, :], ssq[:, 0, i:i + 1])
                s.activation(ssq[:, 1, i:i + 1], ssq[:, 0, i:i + 1], ACT.Sqrt, bias=eps[:, 0:1], scale=1.0 / D).then_inc(e_rms, 1)

            def pre_norm(i):
                act.wait_ge(x2_done, i + 1)
                square_sum(x2[:, i, :], ssq[:, 2, i:i + 1])
                s.activation(ssq[:, 3, i:i + 1], ssq[:, 2, i:i + 1], ACT.Sqrt, bias=eps[:, 0:1], scale=1.0 / D).then_inc(n_rms, 1)

            def h2_columns(i):
                act.wait_ge(h2_done, i + 1)
                act.dma_start(h2_d[i * P:(i + 1) * P, :], h2[i % 3][:, :]).then_inc(h2_out[i], 16)
                act.wait_ge(h2_tr, i + 1)
                if i:
                    act.wait_ge(lg_ps, i)
                s.activation(hfT[:, :, :], ps[:, 2 * i:2 * i + 2, :].rearrange("p b (k n) -> p (b k) n", n=P), ACT.Copy).then_inc(hfT_done, 1)

            post_norm(0)
            post_norm(1)
            for i in range(TT):
                pre_norm(i)
                if i + 2 < TT:
                    post_norm(i + 2)
                if i == TT - 1:
                    act.dma_start(x2_d.rearrange("(i p) d -> p i d", p=P), x2[:, :, :]).then_inc(x2_out, 16)
                if i:
                    h2_columns(i - 1)
            h2_columns(TT - 1)
            act.wait_ge(wsub, 1)
            for i in range(TT):
                s.activation(topw[:, i, :], topw[:, i, :], ACT.Exp, accum_out=ssq[:, 0, i:i + 1]).then_inc(wexp, 1)

            def hi_x(b, half):
                act.wait_ge(xT_ps, b * 2 + (half + 1))
                s.activation(xT[0][:, 4 * half:4 * half + 4, :], ps[:, 6 + half, :].rearrange("p (k n) -> p k n", n=P), ACT.Copy).then_inc(xT_hi, 1)

            def hi_w(b, i):
                act.wait_ge(chunk_in[i], b * 16 + 16 * (mix_uses[i] + 1))
                act.wait_ge(chunk_used, b * MS + (W_MIX + i - HS + 1))
                s.activation(hi[i % HS][:, :], raw[i][:, :], ACT.Copy).then_inc(hi_done, 1)

            def sigmoid(b, half):
                act.wait_ge(chunk_used, b * MS + (W_MIX + 4 * half + 2))
                if half:
                    act.wait_ge(glu_done, b * 2 + 1)
                s.activation(sg[:, :], ps[:, 2 * half, :], ACT.Sigmoid, scale=ALPHA).then_inc(sg_done, 1)

            def hi_a(b, half):
                act.wait_ge(aT_ps, b * 2 + (half + 1))
                s.activation(aT[0][:, 4 * half:4 * half + 4, :], ps[:, 6 + half, :].rearrange("p (k n) -> p k n", n=P), ACT.Copy).then_inc(aT_hi, 1)

            def iteration(b, more):
                for i in range(3, MS):
                    hi_w(b, i)
                    if i == 5:
                        sigmoid(b, 0)
                    if i == 8:
                        hi_a(b, 0)
                        sigmoid(b, 1)
                hi_a(b, 1)
                hi_x(b + 1, 0)
                hi_x(b + 1, 1)

                def next_three():
                    for i in range(3):
                        hi_w(b + 1, i)
                more(next_three)
                act.wait_ge(ysb_free, b + 1)
                act.wait_ge(chunk_used, b * MS + (W_MIX + MS))
                s.activation(ysb[:, :].rearrange("p (h n) -> p h n", h=2), ps[:, 4:6, :], ACT.Copy).then_inc(y_done, 1)

            s.activation(small[:, 61:62], eps[:, :], ACT.Copy).then_inc(y_done, 1)
            for i in range(3):
                hi_w(0, i)
            hi_x(0, 0)
            hi_x(0, 1)
            with act.Fori(0, N_FIRST) as b:
                iteration(b, lambda f: f())
            act.wait_ge(over_done, 1)
            n_last = act.value_load(over_i[0:1, N_LAST + 1:N_LAST + 2], min_val=1, max_val=N_LAST)
            with act.Fori(0, N_LAST) as t:
                with act.If(n_last > t):
                    def if_more(f):
                        with act.If(n_last > t + 1):
                            f()
                    iteration(t + N_FIRST, if_more)
            for i in range(TT):
                act.wait_ge(comb_done, i + 1)
                s.activation(tjunk[:, :], comb[:, i, :], ACT.Square, accum_out=ssq[:, 0, i:i + 1]).then_inc(t_ssq, 1)
                act.wait_ge(t_ssq, 2 * i + 1)
                s.activation(ssq[:, 1, i:i + 1], ssq[:, 0, i:i + 1], ACT.Sqrt, bias=eps[:, 0:1], scale=1.0 / D).then_inc(t_ssq, 1)

        @block.vector
        def _(dve):
            v = nc.vector
            step = Steps(dve, dve_step)
            link = step.link
            done_items = [0]

            def col(r):
                return cols[:, r:r + 1]

            def adaln_sum():
                n = done_items[0]
                done_items[0] += 1
                q = ADAS.index(n)
                part, k = STREAM[n][1], STREAM[n][2]
                dve.wait_ge(chunk_in[n % RS], 16 * (n // RS + 1))
                if k == 0:
                    dve.wait_ge(acc_in[part], 16)
                else:
                    dve.wait_ge(ada_used, q)
                v.scalar_tensor_tensor(out=acc[part][:, :], in0=raw[n % RS][:, :], scalar=scol[:, k:k + 1],
                                       in1=acc[part][:, :], op0=ALU.mult, op1=ALU.add).then_inc(ada_used, 1)

            def advance(w):
                while w < W_MIX and done_items[0] <= WEIGHTS[w]:
                    n = done_items[0]
                    it, r = STREAM[n], raw[n % RS]
                    if it[0] == "ada":
                        adaln_sum()
                    else:
                        done_items[0] += 1
                        ww = WEIGHTS.index(n)
                        c = words(it)
                        dve.wait_ge(hi_done, ww + 1)
                        v.tensor_tensor(lo[n % RS][:, 0:c], r[:, 0:c], hi[hi_slot(ww)][:, 0:c].bitcast(F32),
                                        ALU.subtract).then_inc(split_done, 1)

            dve.wait_ge(cols_ps, 1)
            v.tensor_copy(cols[:, :], ps[:, 7, 0:R_END]).then_inc(cols_done, 1)
            dve.wait_ge(cols_done, 1)
            dve.wait_ge(cexp, 1)
            link(v.tensor_scalar(small[:, 0:8], small[:, 0:8], 1.0, None, ALU.add))
            link(v.reciprocal(small[:, 0:8], small[:, 0:8]))
            v.tensor_tensor(scol[:, :], cols[:, R_C:R_C + 8], small[:, 0:8], ALU.mult).then_inc(scol_done, 1)
            link(v.tensor_scalar(small[:, 30:40], cols[:, R_LAM:R_LAM + MT], -1.0, None, ALU.mult))
            v.tensor_tensor(small[:, 10:20], small[:, 30:40], cols[:, R_LAM:R_LAM + MT], ALU.max).then_inc(sp_exp, 1)
            link(v.tensor_scalar(small[:, 30:40], small[:, 30:40], 0.0, None, ALU.max))
            v.tensor_scalar(bcol[:, 0:16], cols[:, R_BMG:R_BMG + 16], 0.5, None, ALU.mult)
            v.tensor_scalar(bcol[:, 16:26], cols[:, R_BA:R_BA + MT], 0.5, None, ALU.mult)
            link(v.tensor_scalar(bcol[:, 26:36], cols[:, R_BX:R_BX + MT], 0.5, None, ALU.mult))
            dve.wait_ge(scol_done, 1)
            for k in range(KT):
                if k == KT // 2:
                    dve.wait_ge(rms_done, 1)
                    link(v.reciprocal(ssq[:, 1, :], ssq[:, 1, :]))
                    for i in range(TT):
                        v.tensor_scalar(xt[:, i, :], xt[:, i, :], ssq[:, 1, i:i + 1], None, ALU.mult).then_inc(xn_done, 1)
                adaln_sum()
            advance(0)
            dve.wait_ge(mod_ps, 1)
            link(v.tensor_copy(modc[:, 0, :], ps[:, 6, 0:KT]))
            link(v.tensor_scalar(modc[:, 1, :], ps[:, 6, KT:2 * KT], 1.0, None, ALU.add))
            v.tensor_tensor(modc[:, 1, :], modc[:, 1, :], cols[:, R_GPM:R_GPM + KT], ALU.mult).then_inc(mod_done, 1)
            dve.wait_ge(mod_done, 1)
            for k in range(KT + 1):
                if k < KT:
                    dve.wait_ge(tr_done, k + 1)
                    if k >= 2:
                        dve.wait_ge(hT_hi, k - 1)
                        dve.wait_ge(hT_done, k - 1)
                    v.tensor_scalar(htmp[:, k % 2, :], ps[:, 2 + k % 4, :], modc[:, 1, k:k + 1], modc[:, 0, k:k + 1],
                                    ALU.mult, ALU.add).then_inc(htmp_done, 1)
                if k:
                    dve.wait_ge(htmp_done, k)
                    dve.wait_ge(hT_hi, k)
                    ins = v.tensor_tensor(hT[1][:, k - 1, :], htmp[:, (k - 1) % 2, :], hT[0][:, k - 1, :].bitcast(F32), ALU.subtract)
                    ins.then_inc(hT_done, 1)

            def conv(m):
                if m == 0:
                    dve.wait_ge(gw_zero, 3)
                dve.wait_ge(xrp_done, m + 1)
                x_, w_ = xc[:, (m + 2) % 6, :], [col(R_CONVW + t * MT + m) for t in range(CONV)]
                link(v.tensor_scalar(x_, xrp[:, 0:SEQ], w_[0], col(R_CONVB + m), ALU.mult, ALU.add))
                for t in range(1, CONV):
                    ins = v.scalar_tensor_tensor(out=x_, in0=xrp[:, t:t + SEQ], scalar=w_[t], in1=x_, op0=ALU.mult, op1=ALU.add)
                    if t < CONV - 1:
                        link(ins)
                ins.then_inc(conv_done, 1)

            advance(1)
            conv(0)
            conv(1)
            advance(3)
            dve.wait_ge(cexp, 2)
            e_, z_, z2_, p_ = small[:, 20:30], small[:, 40:50], small[:, 50:60], small[:, 10:20]
            link(v.tensor_scalar(z_, e_, 2.0, None, ALU.add))
            link(v.reciprocal(z_, z_))
            link(v.tensor_tensor(z_, z_, e_, ALU.mult))
            link(v.tensor_tensor(z2_, z_, z_, ALU.mult))
            link(v.tensor_scalar(p_, z2_, 1.0 / 17, 1.0 / 15, ALU.mult, ALU.add))
            for t in (13, 11, 9, 7, 5, 3, 1):
                link(v.tensor_tensor(p_, p_, z2_, ALU.mult))
                link(v.tensor_scalar(p_, p_, 1.0 / t, None, ALU.add))
            link(v.tensor_tensor(p_, p_, z_, ALU.mult))
            link(v.scalar_tensor_tensor(out=p_, in0=p_, scalar=2.0, in1=small[:, 30:40], op0=ALU.mult, op1=ALU.add))
            v.tensor_scalar(sp4[:, 0, :], p_, 4.0, None, ALU.mult)
            v.tensor_scalar(sp4[:, 1, :], p_, -4.0, None, ALU.mult).then_inc(sp_done, 1)
            for j in range(MT // 2):
                if 2 * j + 2 < MT:
                    conv(2 * j + 2)
                    conv(2 * j + 3)
                for m in READY[j]:
                    gb, g_ = ps[:, 4 + m % 4, :], g2[:, m % 2, :]
                    dve.wait_ge(g2_done, m + 1)
                    link(v.scalar_tensor_tensor(out=g_, in0=g_, scalar=0.044715, in1=gb, op0=ALU.mult, op1=ALU.mult))
                    v.tensor_tensor(g_, g_, gb, ALU.add).then_inc(inner_done, 1)
                    if j < MT // 2 - 1 and STREAM[done_items[0]][0] == "ada":
                        adaln_sum()
                    dve.wait_ge(a_done, 3 * m + 3)
                    v.scalar_tensor_tensor(out=t_om[:, :], in0=th_a[:, :], scalar=1.0, in1=t_om[:, :], op0=ALU.add, op1=ALU.mult).then_inc(om_done, 1)
                    dve.wait_ge(gates_read, 2 * m + 2)
                    dve.wait_ge(conv_done, m + 1)
                    v.scalar_tensor_tensor(out=th_i[:, :], in0=th_i[:, :], scalar=1.0, in1=xc[:, (m + 2) % 6, :], op0=ALU.add, op1=ALU.mult)
                    dve.wait_ge(gelu_th, m + 1)
                    v.scalar_tensor_tensor(out=g_, in0=g_, scalar=1.0, in1=gb, op0=ALU.add, op1=ALU.mult).then_inc(gelu_done, 1)
                    dve.wait_ge(gelu_done, m + 1)
                    dve.wait_ge(sqrt_done, m + 1)
                    link(v.scalar_tensor_tensor(out=th_i[:, :], in0=th_i[:, :], scalar=0.5, in1=t_om[:, :], op0=ALU.mult, op1=ALU.mult))
                    link(v.tensor_tensor_scan(out=th_a[:, :], data0=dec[:, :], data1=th_i[:, :], initial=0.0, op0=ALU.mult, op1=ALU.add))
                    v.scalar_tensor_tensor(out=g_, in0=g_, scalar=0.5, in1=th_a[:, :], op0=ALU.mult, op1=ALU.mult).then_inc(rnn_done, 1)
                    dve.wait_ge(rnn_done, m + 1)
                    dve.wait_ge(rnn_hi, m + 1)
                    v.tensor_tensor(rnnT[1][:, m, :], g_, rnnT[0][:, m, :].bitcast(F32), ALU.subtract).then_inc(rnn_lo, 1)
                    if m == READY[j][0] and j < MT // 2 - 1:
                        advance(2 * j + 4)
                    if m == READY[j][-1] and j < MT // 2 - 1:
                        advance(2 * j + 5)
                    if m == MT - 2:
                        advance(BR_PROJ[0])

            dve.wait_ge(gpost_in, 48)
            for p in range(4):
                advance(min(BR_PROJ[0] + 3 * p + 2, W_KV))
                for t in (2 * p, 2 * p + 1):
                    dve.wait_ge(bg_done, t + 1)
                    tile_ready(dve, bp_ps, t, BR_PROJ[p] + 1)
                    v.scalar_tensor_tensor(out=mix[:, t, :], in0=gate_s[:, t % 2, :], scalar=1.0,
                                           in1=ps[:, proj_bank(t), :], op0=ALU.add, op1=ALU.mult).then_inc(bm_done, 1)
            for q in range(8):
                dve.wait_ge(mod_ps, 2 + q)
                h = slice(512 * (q % 2), 512 * (q % 2) + 512)
                if q < 2:
                    ins = v.tensor_tensor(gate_m[:, h], gate_m[:, h], ps[:, q, :], ALU.mult)
                elif q < 4:
                    ins = v.tensor_copy(shift_f[:, h], ps[:, q, :])
                elif q < 6:
                    ins = v.scalar_tensor_tensor(out=scale_f[:, h], in0=ps[:, q, :], scalar=1.0, in1=scale_f[:, h], op0=ALU.add, op1=ALU.mult)
                else:
                    ins = v.tensor_tensor(gate_f[:, h], gate_f[:, h], ps[:, q, :], ALU.mult)
                ins.then_inc(mod_done, 1)

            advance(W_KV + 1)
            dve.wait_ge(pos_in, 16)
            dve.wait_ge(small_in, 48)
            dve.wait_ge(mod_done, 9)
            ang, turns = prob[:, 0, :, :].rearrange("p a b -> p (a b)"), prob[:, 1, :, :].rearrange("p a b -> p (a b)")
            link(v.tensor_copy(ang, kpos[:, :]))
            link(v.tensor_scalar(ang, ang, freq[:, 0:1], None, ALU.mult))
            MAGIC, C1 = 12582912.0, 6.28125
            C2, C3 = 0.0019350051879882812, 3.0199157663854277e-07
            for r, quarter in ((cos, 0.25), (sin, 0.0)):
                link(v.tensor_scalar(turns, ang, 0.15915494309189535, quarter, ALU.mult, ALU.add))
                link(v.tensor_scalar(turns, turns, MAGIC, None, ALU.add))
                link(v.tensor_scalar(turns, turns, MAGIC, None, ALU.subtract))
                link(v.scalar_tensor_tensor(out=r[:, :], in0=turns, scalar=-C1, in1=ang, op0=ALU.mult, op1=ALU.add))
                link(v.scalar_tensor_tensor(out=r[:, :], in0=turns, scalar=-C2, in1=r[:, :], op0=ALU.mult, op1=ALU.add))
                link(v.scalar_tensor_tensor(out=r[:, :], in0=turns, scalar=-C3, in1=r[:, :], op0=ALU.mult, op1=ALU.add))
                if quarter:
                    link(v.tensor_scalar(r[:, :], r[:, :], 1.5707963267948966, None, ALU.add))
                v.tensor_scalar(r[:, :], r[:, :], 3.1415925, -3.1415925, ALU.min, ALU.max).then_inc(ang_done, 1)
            dve.wait_ge(trig_done, 2)
            for h in range(2):
                ins = v.tensor_scalar(sin[64 * h:64 * h + 32, :], sin[64 * h:64 * h + 32, :], -1.0, None, ALU.mult)
            link(ins)

            def rotate(bank, r):
                v.tensor_tensor(rot[:, r, :], ps[:, bank, :], cos[:, :], ALU.mult)
                link(v.tensor_tensor(swp[:, r, :], swp[:, r, :], sin[:, :], ALU.mult))

            dve.wait_ge(kv_ps, 1)
            dve.wait_ge(swp_done, 1)
            rotate(0, 0)
            v.tensor_tensor(rot[:, 0, :], rot[:, 0, :], swp[:, 0, :], ALU.add).then_inc(rope_done, 1)
            advance(W_Q + 2)

            def rotate_q(t):
                if t == 0:
                    dve.wait_ge(qbd_zero, 2)
                if t == 1:
                    dve.wait_ge(kT_done, 4)
                tile_ready(dve, q_ps, t, W_Q + t // 2)
                dve.wait_ge(swp_done, t + 2)
                if t:
                    dve.wait_ge(rope_done, t)
                r = (t + 1) % 2
                rotate(q_bank(t), r)
                for h in range(2):
                    hs = slice(64 * h, 64 * h + 64)
                    ins = v.tensor_tensor(qbd[hs, t, :, h, :], rot[hs, r, :].rearrange("p (c q) -> p c q", q=CHUNK),
                                          swp[hs, r, :].rearrange("p (c q) -> p c q", q=CHUNK), ALU.add)
                ins.then_inc(rope_done, 1)

            for t in range(4):
                rotate_q(t)
                if t == 1:
                    advance(W_Q + 3)
            for step_ in range(NU + 3):
                u = step_
                if u < NU:
                    g_ = u // NC
                    n = CHUNK if u % NC == 0 else 2 * CHUNK
                    o = 8 * (u % 2)
                    dve.wait_ge(s_ps, u + 1)
                    if u:
                        dve.wait_ge(m_done, u)
                    if u >= 2:
                        dve.wait_ge(e_done, u - 1)
                        dve.wait_ge(p_done, u - 1)
                    link(v.tensor_reduce(small[:, 48:52], ps[:, u % 2, :].rearrange("p (j n) -> p j n", n=P)[:, :, 0:n], AX_X, ALU.max))
                    link(v.scalar_tensor_tensor(out=small[:, 48:52], in0=small[:, 48:52], scalar=HD ** -0.5,
                                                in1=sink[:, 4 * g_:4 * g_ + 4], op0=ALU.mult, op1=ALU.max))
                    v.tensor_scalar(small[:, o:o + 4], small[:, 48:52], -1.0, None, ALU.mult)
                    v.tensor_tensor(small[:, o + 4:o + 8], sink[:, 4 * g_:4 * g_ + 4], small[:, 48:52], ALU.subtract).then_inc(m_done, 1)
                u = step_ - 1
                if 0 <= u < NU:
                    n = CHUNK if u % NC == 0 else 2 * CHUNK
                    o = 8 * (u % 2)
                    dve.wait_ge(e_done, u + 1)
                    if u:
                        dve.wait_ge(p_done, u)
                    link(v.tensor_tensor(small[:, 52:56], small[:, 16 + o:20 + o], small[:, 32 + o:36 + o], ALU.add))
                    link(v.reciprocal(small[:, 52:56], small[:, 52:56]))
                    v.tensor_tensor(prob[:, u % 2, :, 0:n], prob[:, u % 2, :, 0:n],
                                    small[:, 52:56].unsqueeze(2).to_broadcast([P, 4, n]), ALU.mult).then_inc(p_done, 1)
                u = step_ - 3
                if u >= 0:
                    g_, c = u // NC, u % NC
                    dve.wait_ge(o_hi, 2 * u + 2)
                    for h in range(2):
                        hs = slice(64 * h, 64 * h + 64)
                        ins = v.tensor_tensor(attn[hs, 4 * g_:4 * g_ + 4, c, 1, :],
                                              ps[hs, 4 + u % 2, :].rearrange("p (j h q) -> p j h q", h=2, q=CHUNK)[:, :, h, :],
                                              attn[hs, 4 * g_:4 * g_ + 4, c, 0, :].bitcast(F32), ALU.subtract)
                    ins.then_inc(o_done, 1)
                if step_ in SPLIT_AT:
                    advance(SPLIT_AT[step_])
                what, t = FILL.get(step_ - 1, (None, 0))
                if what == "q":
                    rotate_q(t)
            advance(W_BA + 3)

            for t in range(KT):
                dve.wait_ge(bg_done, KT + t + 1)
                if t >= 2:
                    dve.wait_ge(mrg_done, t - 1)
                tile_ready(dve, ap_ps, t, W_BA + t // 2)
                link(v.scalar_tensor_tensor(out=mtmp[:, t % 2, :], in0=gate_a[:, t, :], scalar=1.0,
                                            in1=ps[:, t % 4, :], op0=ALU.add, op1=ALU.mult))
                v.tensor_tensor(mtmp[:, t % 2, :], mtmp[:, t % 2, :], mix[:, t, :], ALU.add).then_inc(mrg_sum, 1)
                dve.wait_ge(mrg_hi, t + 1)
                v.scalar_tensor_tensor(out=mrgT[1][:, t, :], in0=mtmp[:, t % 2, :], scalar=0.5,
                                       in1=mrgT[0][:, t, :].bitcast(F32), op0=ALU.mult, op1=ALU.subtract).then_inc(mrg_done, 1)
                if t % 2 and t >= 3:
                    advance(W_OUT + t // 2 - 1)
            advance(W_MIX - 1)

            dve.wait_ge(bt_in, 64)
            for part in range(3):
                link(v.tensor_copy(bt16[:, :], btab[:, :]))
                link(v.tensor_copy(bpart[NE * part:NE * part + NE, :], bt16[:, :]))
                if part < 2:
                    link(v.tensor_tensor(btab[:, :], btab[:, :], bt16[:, :], ALU.subtract))
            for part in range(3):
                q = slice(NE * part, NE * part + NE)
                link(v.tensor_copy(onehot[q, :], ident[q, q]))
            v.tensor_copy(sel[:, :], onehot[:, 0:1].to_broadcast([3 * NE, P])).then_inc(sel_done, 1)
            v.memset(over_f[:, :], float(NE - 1)).then_inc(bpart_done, 1)

            dve.wait_ge(xe_in, 16)
            lg, oh, prod = route[:, 0:TT, :], ohe[:, 0, :, :], ohe[:, 1, :, :]
            mask, q0, q1, blk = (route[:, 4 * t:4 * t + 4, :] for t in range(1, 5))
            cnt, nb, incl, basep = (route[:, 20 + t, :] for t in range(4))
            iota_e = iota_f[:, 0:NE]

            def residual(i):
                dve.wait_ge(e_rms, i + 1)
                if i:
                    dve.wait_ge(x2_done, i)
                link(v.reciprocal(ssq[:, 1, i:i + 1], ssq[:, 1, i:i + 1]))
                link(v.scalar_tensor_tensor(out=mixed[:, :], in0=ps[:, 2 * i:2 * i + 2, :].rearrange("p b n -> p (b n)"),
                                            scalar=ssq[:, 1, i:i + 1], in1=gate_m[:, :], op0=ALU.mult, op1=ALU.mult))
                v.tensor_tensor(x2[:, i, :], x2[:, i, :], mixed[:, :], ALU.add).then_inc(x2_done, 1)

            def modulate(i):
                dve.wait_ge(n_rms, i + 1)
                if i >= 3:
                    dve.wait_ge(h2_tr, i - 2)
                    dve.wait_ge(h2_out[i - 3], 16)
                link(v.reciprocal(ssq[:, 3, i:i + 1], ssq[:, 3, i:i + 1]))
                link(v.scalar_tensor_tensor(out=h2[i % 3][:, :], in0=x2[:, i, :], scalar=ssq[:, 3, i:i + 1], in1=scale_f[:, :],
                                            op0=ALU.mult, op1=ALU.mult))
                v.tensor_tensor(h2[i % 3][:, :], h2[i % 3][:, :], shift_f[:, :], ALU.add).then_inc(h2_done, 1)

            def choose(i):
                dve.wait_ge(lg_ps, i + 1)
                link(v.tensor_tensor(lg[:, i, :], ps[:, 2 * i, 0:NE], brt[:, :], ALU.add))
                link(v.max(top8[:, i, :], lg[:, i, :]))
                link(v.max_index(idx8[:, i, :], top8[:, i, :], lg[:, i, :]))

            residual(0)
            residual(1)
            for i in range(TT):
                modulate(i)
                if i + 2 < TT:
                    residual(i + 2)
                if i == TT - 2:
                    choose(0)
            for i in range(1, TT):
                choose(i)
            link(v.tensor_copy(idxf[:, :, :], idx8[:, :, :]))
            for k in range(TOPK):
                ins = v.tensor_tensor(oh[:, TT * k:TT * k + TT, :], iota_e.unsqueeze(1).to_broadcast([P, TT, NE]),
                                      idxf[:, :, k:k + 1].to_broadcast([P, TT, NE]), ALU.is_equal)
            link(ins)
            link(v.tensor_tensor(mask, oh[:, 0:TT, :], oh[:, TT:2 * TT, :], ALU.add))
            link(v.tensor_tensor(mask, mask, oh[:, 2 * TT:3 * TT, :], ALU.add))
            v.tensor_tensor(mask, mask, oh[:, 3 * TT:4 * TT, :], ALU.add).then_inc(mask_done, 1)
            for i in range(TT):
                ins = v.tensor_scalar(topw[:, i, :], top8[:, i, 0:TOPK], top8[:, i, 0:1], None, ALU.subtract)
            ins.then_inc(wsub, 1)
            dve.wait_ge(rank_ps, 1)
            link(v.tensor_copy(cnt, ps[:, 1, 0:NE]))
            link(v.tensor_scalar(nb, cnt, float(P + 1), None, ALU.is_ge))
            for t in (2, 3):
                link(v.scalar_tensor_tensor(out=nb, in0=cnt, scalar=float(t * P + 1), in1=nb, op0=ALU.is_ge, op1=ALU.add))
            link(v.tensor_tensor_scan(out=incl, data0=ones[:, 0:NE], data1=nb, initial=0.0, op0=ALU.mult, op1=ALU.add))
            link(v.scalar_tensor_tensor(out=basep, in0=incl, scalar=float(NE - 1), in1=nb, op0=ALU.add, op1=ALU.subtract))
            link(v.tensor_tensor(basep, basep, iota_e, ALU.subtract))
            rank = ps[:, 0, 0:TT * NE].rearrange("p (i e) -> p i e", e=NE)
            link(v.tensor_scalar(q0, rank, float(P), None, ALU.is_ge))
            link(v.scalar_tensor_tensor(out=q1, in0=rank, scalar=float(2 * P), in1=q0, op0=ALU.is_ge, op1=ALU.add))
            link(v.scalar_tensor_tensor(out=q1, in0=rank, scalar=float(3 * P), in1=q1, op0=ALU.is_ge, op1=ALU.add))
            link(v.tensor_tensor(blk, q0, basep.unsqueeze(1).to_broadcast([P, TT, NE]), ALU.mult))
            link(v.tensor_tensor(blk, blk, iota_e.unsqueeze(1).to_broadcast([P, TT, NE]), ALU.add))
            link(v.tensor_tensor(blk, blk, q1, ALU.add))
            link(v.scalar_tensor_tensor(out=q0, in0=q1, scalar=-float(P), in1=rank, op0=ALU.mult, op1=ALU.add))
            for t, val in ((0, blk), (1, q0)):
                for k in range(TOPK):
                    ins = v.tensor_tensor(prod[:, TT * k:TT * k + TT, :], oh[:, TT * k:TT * k + TT, :], val, ALU.mult)
                link(ins)
                link(v.tensor_reduce(pick[:, t, :], prod, AX_X, ALU.add))
            dve.wait_ge(x2_out, 16)
            for q in range(TOPK * TT):
                v.tensor_scalar(oh_slot[:, q, :], iota_f[:, :], pick[:, 1, q:q + 1], None, ALU.is_equal)
                v.tensor_scalar(oh_blk[:, q, 0:N_BLOCKS + 1], iota_f[:, 0:N_BLOCKS + 1], pick[:, 0, q:q + 1],
                                asgv[:, q // TT, q % TT:q % TT + 1], ALU.is_equal, ALU.mult).then_inc(oh_done, 1)
            dve.wait_ge(tab_ps, 1)
            n_ = N_BLOCKS + 1
            link(v.tensor_scalar(tabf[:, 0, 0:n_], ps[:, 2, 0:n_], 0.0, float(NOWHERE), ALU.is_equal, ALU.mult))
            link(v.scalar_tensor_tensor(out=tabf[:, 1, 0:n_], in0=ps[:, 2, 0:n_], scalar=-1.0, in1=tabf[:, 0, 0:n_], op0=ALU.add, op1=ALU.add))
            link(v.tensor_copy(asg_i[:, :], tabf[:, 1, 0:n_]))
            v.tensor_scalar(tok_i[:, :], asg_i[:, :], 2, None, ALU.arith_shift_right).then_inc(tab_done, 1)

            for o in range(N_OVER):
                ins = v.tensor_scalar(route[:, 24 + o, :], incl, float(o), None, ALU.is_le)
            link(ins)
            link(v.tensor_reduce(over_f[:, 1:N_OVER + 1], route[:, 24:24 + N_OVER, :], AX_X, ALU.add))
            link(v.tensor_scalar(over_f[:, 1:N_OVER + 1], over_f[:, 1:N_OVER + 1], float(NE - 1), None, ALU.min))
            link(v.tensor_scalar(over_f[:, N_LAST + 1:N_LAST + 2], incl[:, NE - 1:NE], 1.0, None, ALU.add))
            v.tensor_copy(over_i[:, :], over_f[:, :]).then_inc(over_done, 1)
            dve.wait_ge(wexp, TT)
            link(v.reciprocal(ssq[:, 0, :], ssq[:, 0, :]))
            link(v.tensor_tensor(topw[:, :, :], topw[:, :, :], ssq[:, 0, :].unsqueeze(2).to_broadcast([P, TT, TOPK]), ALU.mult))

            def lo_w(b, i):
                dve.wait_ge(hi_done, b * MS + (W_MIX + i + 1))
                v.tensor_tensor(lo[i][:, :], raw[i][:, :], hi[i % HS][:, :].bitcast(F32), ALU.subtract).then_inc(split_done, 1)

            def lo_x(b, half):
                dve.wait_ge(xT_hi, b * 2 + (half + 1))
                h = slice(4 * half, 4 * half + 4)
                v.tensor_tensor(xT[1][:, h, :], ps[:, 6 + half, :].rearrange("p (k n) -> p k n", n=P),
                                xT[0][:, h, :].bitcast(F32), ALU.subtract).then_inc(xT_done, 1)

            def lo_a(b, half):
                dve.wait_ge(aT_hi, b * 2 + (half + 1))
                h = slice(4 * half, 4 * half + 4)
                v.tensor_tensor(aT[1][:, h, :], ps[:, 6 + half, :].rearrange("p (k n) -> p k n", n=P),
                                aT[0][:, h, :].bitcast(F32), ALU.subtract).then_inc(aT_done, 1)

            def glu_gate(b, half, st):
                dve.wait_ge(sg_done, b * 2 + (half + 1))
                if half:
                    dve.wait_ge(glu_done, b * 2 + 1)
                st(v.tensor_scalar(gmin[:, :], ps[:, 2 * half, :], LIMIT, None, ALU.min))
                st.wait()
                st(v.scalar_tensor_tensor(out=gmin[:, :], in0=sg[:, :], scalar=SIG_LIMIT, in1=gmin[:, :], op0=ALU.min, op1=ALU.mult))

            def glu_up(b, half, st):
                dve.wait_ge(chunk_used, b * MS + (W_MIX + 4 * half + 4))
                st(v.tensor_scalar(ucl[:, :], ps[:, 2 * half + 1, :], LIMIT, -LIMIT, ALU.min, ALU.max))
                st.wait()
                v.scalar_tensor_tensor(out=act_h[:, half, :], in0=ucl[:, :], scalar=1.0, in1=gmin[:, :], op0=ALU.add, op1=ALU.mult).then_inc(glu_done, 1)

            st = Steps(dve, glu_step)

            def iteration(b, next_expert, more):
                st.n, st.at = 0, b * 6
                for i in range(3, MS):
                    if i == MS - 1:
                        lo_a(b, 1)
                    lo_w(b, i)
                    if i == 5:
                        glu_gate(b, 0, st)
                    if i == 6:
                        glu_up(b, 0, st)
                    if i == 8:
                        lo_a(b, 0)
                    if i == 9:
                        glu_gate(b, 1, st)
                        glu_up(b, 1, st)
                lo_x(b + 1, 0)
                v.tensor_copy(sel[:, :], onehot[:, bass.DynSlice(next_expert(), 1)].to_broadcast([3 * NE, P])).then_inc(sel_done, 1)
                lo_x(b + 1, 1)

                def next_three():
                    for i in range(3):
                        lo_w(b + 1, i)
                more(next_three)

            for i in range(3):
                lo_w(0, i)
            lo_x(0, 0)
            lo_x(0, 1)
            with dve.Fori(0, N_FIRST) as b:
                iteration(b, lambda: b + 1, lambda f: f())
            dve.wait_ge(over_done, 1)
            n_last = dve.value_load(over_i[0:1, N_LAST + 1:N_LAST + 2], min_val=1, max_val=N_LAST)
            with dve.Fori(0, N_LAST) as t:
                with dve.If(n_last > t):
                    def if_more(f):
                        with dve.If(n_last > t + 1):
                            f()
                    iteration(t + N_FIRST, lambda: dve.value_load(over_i[0:1, bass.DynSlice(t + 1, 1)], min_val=0, max_val=NE - 1), if_more)

            tl = Steps(dve, tail_step)
            def combine(i):
                c_ = comb[:, i, :]
                dve.wait_ge(yk_in[i], 16)
                tl.link(v.tensor_scalar(c_, yk[:, i, 0, :], topw[:, i, 0:1], None, ALU.mult))
                for k in range(1, TOPK):
                    ins = v.scalar_tensor_tensor(out=c_, in0=yk[:, i, k, :], scalar=topw[:, i, k:k + 1], in1=c_, op0=ALU.mult, op1=ALU.add)
                    if k < TOPK - 1:
                        tl.link(ins)
                ins.then_inc(comb_done, 1)

            def finish(i):
                c_ = comb[:, i, :]
                dve.wait_ge(t_ssq, 2 * i + 2)
                tl.link(v.reciprocal(ssq[:, 1, i:i + 1], ssq[:, 1, i:i + 1]))
                tl.link(v.scalar_tensor_tensor(out=c_, in0=c_, scalar=ssq[:, 1, i:i + 1], in1=gate_f[:, :], op0=ALU.mult, op1=ALU.mult))
                v.tensor_tensor(c_, c_, x2t[i // 2][:, i % 2, :], ALU.add).then_inc(fin_done, 1)

            combine(0)
            dve.wait_ge(x2t_in, 32)
            for i in range(TT):
                if i + 1 < TT:
                    combine(i + 1)
                finish(i)

        @block.tensor
        def _(pe):
            mm = nc.tensor.matmul
            PARTS = ((0, 0), (0, 1), (1, 0))

            def chunk(w):
                pe.wait_ge(split_done, w + 1)
                n = WEIGHTS[w]
                c = words(STREAM[n])
                return hi[hi_slot(w)][:, 0:c], lo[n % RS][:, 0:c]

            def feature_major(bank, parts, c0, acts, k0, kn, start, stop, ready=None):
                for k in range(kn):
                    if ready is not None:
                        pe.wait_ge(ready, k + 1)
                    for q, (xa, wa) in enumerate(PARTS):
                        wk = parts[wa].rearrange("p (k n) -> p k n", k=kn)
                        last = mm(ps[:, bank, :], wk[:, k, c0:c0 + P], acts[xa][:, k0 + k, :],
                                  start=start and k == 0 and q == 0, stop=stop and k == kn - 1 and q == 2)
                return last

            pe.wait_ge(consts, 7)
            pe.wait_ge(rows_in, 16 * 8)
            nc.tensor.transpose(ps[:, 7, 0:R_END], rows[0:R_END, :], ident[0:R_END, 0:R_END]).then_inc(cols_ps, 1)
            pe.wait_ge(xn_done, TT)
            for k in range(KT):
                if k >= 4:
                    pe.wait_ge(htmp_done, k - 3)
                for i in range(TT):
                    last = nc.tensor.transpose(ps[:, 2 + k % 4, i * P:(i + 1) * P], xt[:, i, k * P:(k + 1) * P], ident[:, :])
                last.then_inc(tr_done, 1)
                if k == 3:
                    pe.wait_ge(ada_used, KT)
                    for c in range(2 * KT):
                        last = mm(ps[:, 6, c:c + 1], acc[0][:, c * P:(c + 1) * P], ones[:, 0:1], start=True, stop=True)
                    last.then_inc(mod_ps, 1)

            def x_tiles(j):
                parts = chunk(W_RNN + 2 * j)
                for m in (2 * j, 2 * j + 1):
                    if m >= 2:
                        pe.wait_ge(xrp_done, m - 1)
                    last = feature_major(m % 2, parts, (m % 2) * P, hT, 0, KT, True, True, hT_done if m == 0 else None)
                    last.then_inc(chunk_used if m % 2 else x_ps, 1)

            def g_tile(m):
                parts = chunk(W_RNN + 2 * (m // 2) + 1)
                if m >= 4:
                    pe.wait_ge(gelu_done, m - 3)
                last = feature_major(4 + m % 4, parts, (m % 2) * P, hT, 0, KT, True, True)
                last.then_inc(chunk_used if m % 2 else g_ps, 1)

            def branch_gate_tile(t):
                parts = chunk(BR_GATE[t // 2])
                if t < 2:
                    pe.wait_ge(xrp_done, MT)
                elif t < 4:
                    pe.wait_ge(gelu_done, t + 5)
                else:
                    pe.wait_ge(bg_done, t - 3)
                feature_major(gate_bank(t), parts, (t % 2) * P, hT, 0, KT, True, True).then_inc(chunk_used if t % 2 else bg_ps, 1)

            def branch_gate(p):
                branch_gate_tile(2 * p)
                branch_gate_tile(2 * p + 1)

            x_tiles(0)
            g_tile(0)
            g_tile(1)
            for j in range(MT // 2):
                if j + 1 < MT // 2:
                    x_tiles(j + 1)
                if j == 0:
                    for which in range(2):
                        pe.wait_ge(gw_in[which], 16 * len(GATE_PIECES))
                pe.wait_ge(conv_done, 2 * j + 2)
                for m in READY[j]:
                    if m:
                        pe.wait_ge(gates_read, 2 * m)
                    pairs = [(q, k) for q, (k, mm_) in enumerate(PAIRS) if mm_ == m]
                    for which in range(2):
                        for n, (q, k) in enumerate(pairs):
                            last = mm(ps[:, 2 + which, :], gw[:, which, q, :], xc[:, (k + 2) % 6, :], start=n == 0, stop=n == len(pairs) - 1)
                    last.then_inc(gates_ps, 1)
                    if j + 1 < MT // 2:
                        if m == READY[j][0]:
                            g_tile(2 * j + 2)
                        if m == READY[j][-1]:
                            g_tile(2 * j + 3)
                    if j + 1 == MT // 2 and m < MT - 1:
                        branch_gate_tile(m - READY[j][0])
            branch_gate(1)

            def sums_over_partitions(acc_, bank0):
                for q in range(4):
                    mm(ps[:, bank0 + q, :], ones[:, :], acc_[:, q * 512:(q + 1) * 512], start=True, stop=True).then_inc(mod_ps, 1)

            pe.wait_ge(gates_read, 2 * MT)
            pe.wait_ge(gelu_done, MT)
            for p in range(4):
                for half in range(2):
                    pe.wait_ge(rnn_lo, MT // 2 * (half + 1))
                    parts = chunk(BR_PROJ[p] + half)
                    for t in (2 * p, 2 * p + 1):
                        if half == 0 and t >= 4:
                            pe.wait_ge(bm_done, t - 3)
                        last = feature_major(proj_bank(t), parts, (t % 2) * P, rnnT, half * (MT // 2), MT // 2, half == 0, half == 1)
                        if t % 2 or half:
                            last.then_inc(chunk_used if t % 2 else bp_ps, 1)
                if p + 2 < 4:
                    branch_gate(p + 2)
            pe.wait_ge(ada_used, 2 * KT)
            pe.wait_ge(bm_done, 6)
            sums_over_partitions(acc[1], 0)
            pe.wait_ge(ada_used, 3 * KT)
            pe.wait_ge(bm_done, KT)
            sums_over_partitions(acc[2], 4)

            parts = chunk(W_KV)
            pe.wait_ge(mod_done, 5)
            feature_major(0, parts, 0, hT, 0, KT, True, True).then_inc(kv_ps, 1)
            for b in range(NC - 1):
                bank, c0 = 1 + b // 4, (b % 4) * P
                for k in range(KT):
                    for q, (xa, wa) in enumerate(PARTS):
                        wk = parts[wa].rearrange("p (k n) -> p k n", k=KT)
                        last = mm(ps[:, bank, c0:c0 + P], hT[xa][:, k, CHUNK * b:CHUNK * b + P], wk[:, k, P:2 * P],
                                  start=k == 0 and q == 0, stop=k == KT - 1 and q == 2)
            last.then_inc(chunk_used, 1)

            def q_tile(t):
                parts = chunk(W_Q + t // 2)
                if t == 0:
                    pe.wait_ge(mod_done, 9)
                if t >= 4:
                    pe.wait_ge(rope_done, t)
                feature_major(q_bank(t), parts, (t % 2) * P, hT, 0, KT, True, True).then_inc(chunk_used if t % 2 else q_ps, 1)

            def merge_gate(t):
                parts = chunk(W_MG + t // 2)
                if t < 2:
                    pe.wait_ge(rope_done, KT + t)
                else:
                    pe.wait_ge(bg_done, KT + t - 1)
                feature_major(6 + t % 2, parts, (t % 2) * P, hT, 0, KT, True, True).then_inc(chunk_used if t % 2 else ag_ps, 1)

            for t in range(5):
                q_tile(t)
            for step_ in range(NU + 3):
                u = step_
                if u < NU:
                    g_, c = u // NC, u % NC
                    k0, n = (0, CHUNK) if c == 0 else (CHUNK * (c - 1), 2 * CHUNK)
                    if u == 0:
                        pe.wait_ge(kT_done, 4)
                        pe.wait_ge(v_done, 4)
                    if c == 0:
                        pe.wait_ge(rope_done, 1 + 4 * (g_ + 1))
                    if u >= 2:
                        pe.wait_ge(e_done, u - 1)
                    for jj in range(4):
                        last = mm(ps[:, u % 2, jj * P:jj * P + n], qbd[:, 4 * g_ + jj, c, :, :].rearrange("p h q -> p (h q)"),
                                  kT[:, g_, k0:k0 + n], start=True, stop=True)
                    last.then_inc(s_ps, 1)
                u = step_ - 2
                if 0 <= u < NU:
                    n = CHUNK if u % NC == 0 else 2 * CHUNK
                    pe.wait_ge(p_done, u + 1)
                    if u >= 2:
                        pe.wait_ge(pT_done, u - 1)
                    for jj in range(4):
                        last = nc.tensor.transpose(ps[0:n, 2 + u % 2, jj * P:(jj + 1) * P], prob[:, u % 2, jj, 0:n], ident[:, :])
                    last.then_inc(pT_ps, 1)
                u = step_ - 3
                if u >= 0:
                    g_, c = u // NC, u % NC
                    n = CHUNK if c == 0 else 2 * CHUNK
                    pe.wait_ge(pT_done, u + 1)
                    if u >= 2:
                        pe.wait_ge(o_done, u - 1)
                    mm(ps[:, 4 + u % 2, :], vb[0:n, max(c - 1, 0), g_, :, :].rearrange("p t d -> p (t d)"),
                       probT[0:n, u % 2, :, :].rearrange("p j n -> p (j n)"), start=True, stop=True).then_inc(o_ps, 1)
                what, t = FILL.get(step_, (None, 0))
                if what == "q" and step_:
                    q_tile(t)
                elif what == "mg":
                    merge_gate(t)

            pe.wait_ge(o_done, NU)
            for t in range(KT):
                parts = chunk(W_BA + t // 2)
                if t >= 4:
                    pe.wait_ge(mrg_sum, t - 3)
                for k in range(KT):
                    for q, (xa, wa) in enumerate(PARTS):
                        wk = parts[wa].rearrange("p (k n) -> p k n", k=KT)
                        last = mm(ps[:, t % 4, :].rearrange("p (c q) -> p c q", q=CHUNK), wk[:, k, (t % 2) * P:(t % 2) * P + P],
                                  attn[:, k, :, xa, :], start=k == 0 and q == 0, stop=k == KT - 1 and q == 2)
                last.then_inc(chunk_used if t % 2 else ap_ps, 1)

            for q in range(4):
                parts = chunk(W_OUT + q)
                pe.wait_ge(mrg_done, 2 * q + 2)
                if q == 0:
                    pe.wait_ge(mrg_sum, KT)
                for i in range(TT):
                    for h in range(2):
                        for kk in range(2):
                            for s_, (xa, wa) in enumerate(PARTS):
                                wk = parts[wa].rearrange("p (k n) -> p k n", k=2)
                                last = mm(ps[:, 2 * i + h, :], mrgT[xa][:, 2 * q + kk, i * P:(i + 1) * P], wk[:, kk, h * 512:(h + 1) * 512],
                                          start=q == 0 and kk == 0 and s_ == 0, stop=q == 3 and kk == 1 and s_ == 2,
                                          skip_group_check=True)
                last.then_inc(chunk_used, 1)

            def logits(i):
                pe.wait_ge(hfT_done, i + 1)
                for k in range(KT):
                    last = mm(ps[:, 2 * i, 0:NE], hfT[:, k, :], wr[:, k, :], start=k == 0, stop=k == KT - 1)
                last.then_inc(lg_ps, 1)

            for i in range(TT):
                pe.wait_ge(h2_done, i + 1)
                for k in range(KT):
                    last = nc.tensor.transpose(ps[:, 2 * i + k // 4, (k % 4) * P:(k % 4 + 1) * P], h2[i % 3][:, k * P:(k + 1) * P], ident[:, :])
                last.then_inc(h2_tr, 1)
                if i:
                    logits(i - 1)
            logits(TT - 1)
            pe.wait_ge(mask_done, 1)
            mask = route[:, 4:8, :]
            for i in range(TT):
                for j in range(i + 1):
                    mm(ps[:, 0, i * NE:(i + 1) * NE], before[:, :] if j == i else ones[:, :], mask[:, j, :], start=j == 0, stop=j == i)
            for i in range(TT):
                last = mm(ps[:, 1, 0:NE], ones[:, :], mask[:, i, :], start=i == 0, stop=i == TT - 1)
            last.then_inc(rank_ps, 1)
            for q in range(TOPK * TT):
                pe.wait_ge(oh_done, q + 1)
                last = mm(ps[:, 2, 0:N_BLOCKS + 1], oh_slot[:, q, :], oh_blk[:, q, 0:N_BLOCKS + 1], start=q == 0, stop=q == TOPK * TT - 1)
            last.then_inc(tab_ps, 1)

            def turn_x(half):
                for k in range(4):
                    last = nc.tensor.transpose(ps[:, 6 + half, k * P:(k + 1) * P], xg[:, (4 * half + k) * P:(4 * half + k + 1) * P], ident[:, :])
                last.then_inc(xT_ps, 1)

            def turn_a(half):
                for k in range(4):
                    last = nc.tensor.transpose(ps[:, 6 + half, k * P:(k + 1) * P], act_h[:, half, k * P:(k + 1) * P], ident[:, :])
                last.then_inc(aT_ps, 1)

            def bias(bank, c0):
                mm(ps[:, bank, :], sel[:, :], bpart[:, c0:c0 + 512], start=True, stop=False)

            def expert_parts(i, kn):
                return [t[:, :].rearrange("p (k n) -> p k n", k=kn) for t in (hi[i % HS], lo[i])]

            def iteration(b):
                for i in range(8):
                    half, what, kk = i // 4, (i // 2) % 2, i % 2
                    bank = 2 * half + what
                    if i == 0:
                        pe.wait_ge(sel_done, b + 1)
                        pe.wait_ge(xT_done, b * 2 + 2)
                    pe.wait_ge(split_done, b * MS + (W_MIX + i + 1))
                    if kk == 0:
                        bias(bank, what * DE + half * 512)
                    wk = expert_parts(i, 4)
                    for k in range(4):
                        if i == 6 and k == 2:
                            pe.wait_ge(glu_done, b * 2 + 1)
                            turn_a(0)
                        for q, (xa, wa) in enumerate(PARTS):
                            last = mm(ps[:, bank, :], xT[xa][:, 4 * kk + k, :], wk[wa][:, k, :], start=False, stop=kk == 1 and k == 3 and q == 2)
                    last.then_inc(chunk_used, 1)
                for i in range(8, MS):
                    if i == 8:
                        pe.wait_ge(y_done, b + 1)
                        pe.wait_ge(aT_done, b * 2 + 1)
                        for h in range(2):
                            bias(4 + h, 2 * DE + h * 512)
                    if i == 10:
                        pe.wait_ge(aT_done, b * 2 + 2)
                        turn_x(1)
                    pe.wait_ge(split_done, b * MS + (W_MIX + i + 1))
                    wk = expert_parts(i, 2)
                    for k in range(2):
                        if i == 9 and k == 1:
                            pe.wait_ge(glu_done, b * 2 + 2)
                            turn_a(1)
                        for h in range(2):
                            for q, (xa, wa) in enumerate(PARTS):
                                last = mm(ps[:, 4 + h, :], aT[xa][:, 2 * (i - 8) + k, :], wk[wa][:, k, h * 512:(h + 1) * 512],
                                          start=False, stop=i == MS - 1 and k == 1 and q == 2)
                    last.then_inc(chunk_used, 1)
                    if i == 9:
                        pe.wait_ge(xg_in, b * 16 + 32)
                        turn_x(0)

            pe.wait_ge(xg_in, 16)
            pe.wait_ge(xg_zero, 1)
            turn_x(0)
            turn_x(1)
            with pe.Fori(0, N_FIRST) as b:
                iteration(b)
            pe.wait_ge(over_done, 1)
            n_last = pe.value_load(over_i[0:1, N_LAST + 1:N_LAST + 2], min_val=1, max_val=N_LAST)
            with pe.Fori(0, N_LAST) as t:
                with pe.If(n_last > t):
                    iteration(t + N_FIRST)


_NAMES = ["x", "c", "positions", "w_ada", "b_ada", "g_pre_mix", "g_post_mix", "g_pre_ffn", "g_post_ffn", "w_in", "sinks",
          "conv_w", "conv_b", "w_rg_a", "b_rg_a", "w_rg_x", "b_rg_x", "rg_lambda", "w_branch_attn", "w_branch_rnn",
          "w_merge_gate", "b_merge_gate", "w_out", "w_router", "b_router", "w_e1", "b_e1", "w_e2", "b_e2"]


def kernel(**inputs):
    import numpy as _np
    import concourse.bacc as _bacc
    from concourse import mybir as _mybir
    from concourse.bass_utils import run_bass_kernel_spmd as _run

    nc = _bacc.Bacc("TRN2", target_bir_lowering=False, num_devices=1)
    arrays, args = {}, {}
    for name in _NAMES:
        arrays[name + "_dram"] = _np.ascontiguousarray(inputs[name])
    half = HD // 2
    freq = (10000.0 ** (-_np.arange(half) / half)).astype(_np.float32)
    arrays["inv_freq_dram"] = _np.ascontiguousarray(_np.concatenate([freq] * 4)[:, None])
    for name in _NAMES + ["inv_freq"]:
        arr = arrays[name + "_dram"]
        args[name] = nc.dram_tensor(name + "_dram", arr.shape, _mybir.dt.from_np(arr.dtype), kind="ExternalInput").ap()
    out = nc.dram_tensor("out_dram", (1, SEQ, D), F32, kind="ExternalOutput").ap()
    hybrid_block(nc, args, out)
    r = _run(nc, [arrays], core_ids=[0])
    return r.results[0]["out_dram"]
```
